# Optimizing a Trainium2 kernel written in Bass

```python
import math
import jax, jax.numpy as jnp
from jax import lax
import numpy as np

D_MODEL = 1024
BATCH = 1
SEQ = 256
DEPTH = 1

ATTN_WIDTH = D_MODEL // 2
POOL_WIDTH = D_MODEL - ATTN_WIDTH
HEAD_DIM = 64
N_HEADS = ATTN_WIDTH // HEAD_DIM
MOBA_BLOCK = 256
MOBA_TOPK = 3
Q_CHUNK = 32
POOL_WINDOWS = (2, 4, 8, 16)
N_POOL_GROUPS = len(POOL_WINDOWS)
POOL_GROUP = POOL_WIDTH // N_POOL_GROUPS
ROPE_THETA = 10000.0
EPS = 1e-6
IN_WIDTH = 4 * ATTN_WIDTH + 2 * POOL_WIDTH

kernel_name = "hymba_moba_pool_hybrid"

def rmsnorm(x, g):
    xf = x.astype(jnp.float32)
    y = xf * lax.rsqrt(jnp.mean(xf * xf, axis=-1, keepdims=True) + EPS)
    return (y * g.astype(jnp.float32)).astype(x.dtype)

def rope(x, pos):
    dh = x.shape[-1]
    inv_freq = 1.0 / (ROPE_THETA ** (jnp.arange(0, dh, 2, dtype=jnp.float32) / dh))
    ang = pos[:, None] * inv_freq[None, :]
    cos, sin = jnp.cos(ang), jnp.sin(ang)
    xf = x.astype(jnp.float32)
    x1, x2 = xf[..., : dh // 2], xf[..., dh // 2:]
    out = jnp.concatenate([x1 * cos - x2 * sin, x2 * cos + x1 * sin], axis=-1)
    return out.astype(x.dtype)

def moba_attention(q, k, v):
    B, H, S, dh = q.shape
    nb = -(-S // MOBA_BLOCK)
    s_pad = nb * MOBA_BLOCK
    padw = ((0, 0), (0, 0), (0, s_pad - S), (0, 0))
    q, k, v = jnp.pad(q, padw), jnp.pad(k, padw), jnp.pad(v, padw)
    kb = k.reshape(B, H, nb, MOBA_BLOCK, dh)
    vb = v.reshape(B, H, nb, MOBA_BLOCK, dh)
    k_mean = jnp.mean(kb.astype(jnp.float32), axis=3)
    n_chunks = s_pad // Q_CHUNK
    qc = jnp.transpose(q.reshape(B, H, n_chunks, Q_CHUNK, dh), (2, 0, 1, 3, 4))
    k_sel = min(MOBA_TOPK, nb)
    scale = HEAD_DIM ** -0.5
    bi = jnp.arange(B)[:, None, None, None]
    hi = jnp.arange(H)[None, :, None, None]
    blk_ids = jnp.arange(nb)
    own_off = jnp.arange(MOBA_BLOCK)

    def step(args):
        c, qi = args
        q_start = c * Q_CHUNK
        qpos = q_start + jnp.arange(Q_CHUNK)
        blk = q_start // MOBA_BLOCK
        qf = qi.astype(jnp.float32)
        gate = jnp.einsum('bhqd,bhnd->bhqn', qf, k_mean)
        gate = jnp.where(blk_ids[None, None, None, :] < blk, gate, -jnp.inf)
        _, top_idx = lax.top_k(gate, k_sel)
        sel_valid = top_idx < blk
        ks = kb[bi, hi, top_idx]
        vs = vb[bi, hi, top_idx]
        s_sel = jnp.einsum('bhqd,bhqkjd->bhqkj', qf, ks.astype(jnp.float32)) * scale
        s_sel = jnp.where(sel_valid[..., None], s_sel, -jnp.inf)
        s_sel = s_sel.reshape(B, H, Q_CHUNK, k_sel * MOBA_BLOCK)
        k_own = lax.dynamic_index_in_dim(kb, blk, axis=2, keepdims=False)
        v_own = lax.dynamic_index_in_dim(vb, blk, axis=2, keepdims=False)
        kpos = blk * MOBA_BLOCK + own_off
        s_own = jnp.einsum('bhqd,bhjd->bhqj', qf, k_own.astype(jnp.float32)) * scale
        s_own = jnp.where(kpos[None, :] <= qpos[:, None], s_own, -jnp.inf)
        p = jax.nn.softmax(jnp.concatenate([s_sel, s_own], axis=-1), axis=-1)
        p_sel = p[..., : k_sel * MOBA_BLOCK].reshape(B, H, Q_CHUNK, k_sel, MOBA_BLOCK)
        p_own = p[..., k_sel * MOBA_BLOCK:]
        out = (jnp.einsum('bhqkj,bhqkjd->bhqd', p_sel, vs.astype(jnp.float32))
               + jnp.einsum('bhqj,bhjd->bhqd', p_own, v_own.astype(jnp.float32)))
        return out.astype(qi.dtype)

    outs = lax.map(step, (jnp.arange(n_chunks), qc))
    out = jnp.transpose(outs, (1, 2, 0, 3, 4)).reshape(B, H, s_pad, dh)
    return out[:, :, :S]

def causal_pool_minus_identity(u, window):
    S = u.shape[1]
    cs = jnp.cumsum(u.astype(jnp.float32), axis=1)
    cs_prev = jnp.pad(cs, ((0, 0), (window, 0), (0, 0)))[:, :S]
    count = jnp.minimum(jnp.arange(1, S + 1), window).astype(jnp.float32)[None, :, None]
    mean = (cs - cs_prev) / count
    return (mean - u.astype(jnp.float32)).astype(u.dtype)

def multiscale_pool(u, w_pool, b_pool, pool_scale):
    B, S, _ = u.shape
    ug = u.reshape(B, S, N_POOL_GROUPS, POOL_GROUP)
    pooled = jnp.stack([causal_pool_minus_identity(ug[:, :, g], POOL_WINDOWS[g])
                        for g in range(N_POOL_GROUPS)], axis=2)
    y = jnp.einsum('bsgc,gcd->bsgd', pooled, w_pool) + b_pool
    return y.reshape(B, S, POOL_WIDTH) * pool_scale

def setup_inputs(seed: int = 0) -> dict:
    key = jax.random.key(seed)
    ks = jax.random.split(key, 8)
    f32 = jnp.float32
    x = jax.random.normal(ks[0], (BATCH, SEQ, D_MODEL), f32)
    norm_gain = 1.0 + 0.02 * jax.random.normal(ks[1], (DEPTH, D_MODEL), f32)
    w_in = jax.random.normal(ks[2], (DEPTH, D_MODEL, IN_WIDTH), f32) * D_MODEL ** -0.5
    w_pool = jax.random.normal(ks[3], (DEPTH, N_POOL_GROUPS, POOL_GROUP, POOL_GROUP), f32) * POOL_GROUP ** -0.5
    b_pool = 0.02 * jax.random.normal(ks[4], (DEPTH, N_POOL_GROUPS, POOL_GROUP), f32)
    pool_scale = 1.0 + 0.02 * jax.random.normal(ks[5], (DEPTH, POOL_WIDTH), f32)
    w_out = jax.random.normal(ks[6], (DEPTH, D_MODEL, D_MODEL), f32) * D_MODEL ** -0.5
    final_gain = 1.0 + 0.02 * jax.random.normal(ks[7], (D_MODEL,), f32)
    return {"x": x, "norm_gain": norm_gain, "w_in": w_in, "w_pool": w_pool,
            "b_pool": b_pool, "pool_scale": pool_scale, "w_out": w_out,
            "final_gain": final_gain}

def reference(x, norm_gain, w_in, w_pool, b_pool, pool_scale, w_out, final_gain):
    B, S, _ = x.shape
    pos = jnp.arange(S, dtype=jnp.float32)
    splits = [ATTN_WIDTH, 2 * ATTN_WIDTH, 3 * ATTN_WIDTH, 4 * ATTN_WIDTH,
              4 * ATTN_WIDTH + POOL_WIDTH]
    for l in range(DEPTH):
        h = rmsnorm(x, norm_gain[l])
        proj = h @ w_in[l]
        q, k, v, g_attn, u, g_pool = jnp.split(proj, splits, axis=-1)

        def heads(t):
            return jnp.transpose(t.reshape(B, S, N_HEADS, HEAD_DIM), (0, 2, 1, 3))

        qh, kh, vh = rope(heads(q), pos), rope(heads(k), pos), heads(v)
        attn = moba_attention(qh, kh, vh)
        attn = jnp.transpose(attn, (0, 2, 1, 3)).reshape(B, S, ATTN_WIDTH)
        attn = attn * jax.nn.silu(g_attn)

        pool = multiscale_pool(u, w_pool[l], b_pool[l], pool_scale[l])
        pool = pool * jax.nn.silu(g_pool)

        mixed = jnp.concatenate([attn, pool], axis=-1)
        x = x + mixed @ w_out[l]
    return rmsnorm(x, final_gain)


_drawn_inputs = setup_inputs


def setup_inputs(seed=0):
    import zlib

    import numpy as np

    out = dict(_drawn_inputs(seed))
    spreads = {}
    factors = {'norm_gain': 5.143, 'b_pool': 7.338, 'pool_scale': 8.0, 'final_gain': 2.866}
    for name, (base, spread) in spreads.items():
        noise = np.random.default_rng([zlib.crc32(name.encode()), seed]).standard_normal(out[name].shape)
        drawn = base * np.exp(spread * noise) if base else spread * noise
        out[name] = __import__('jax').numpy.asarray(drawn.astype(out[name].dtype))
    for name, factor in factors.items():
        out[name] = (out[name] * factor).astype(out[name].dtype)
    return out
```

```python
import concourse.bass as bass
from concourse import mybir
from contextlib import ExitStack

import numpy as np

SEQ, D = 256, 1024
HEADS, HEAD_DIM = 8, 64
WIDTH = HEADS * HEAD_DIM
BLOCKS = 6
WINDOWS = (2, 4, 8, 16)
GROUPS = len(WINDOWS)
EPS = 1e-6
THETA = 10000.0
P = 128
KT = D // P
TT = SEQ // P
HALF = HEAD_DIM // 2
WARM_UP = 14
EDGE = max(WINDOWS)


def hymba_kernel(nc, x, x_t, gain, w_in, w_pool, b_pool, pool_scale, w_out, final_gain,
                 rope_table, edge_table, out):
    fp32, fp32r = mybir.dt.float32, mybir.dt.float32r
    ALU, ACT = mybir.AluOpType, mybir.ActivationFunctionType

    ORDER = [0, 1, 2, 4, 3, 5]
    Q, K, V, U, GA, GP = range(BLOCKS)
    CHUNK = 1024
    PER_BLOCK = KT * WIDTH // CHUNK
    IN_CHUNKS = BLOCKS * PER_BLOCK
    CHUNKS = IN_CHUNKS + KT
    RAW, SPLIT = 8, 5
    STEPS = 2 * CHUNKS
    OUT_STEP = 2 * IN_CHUNKS
    AHEAD = 6

    def scores_at(h): return 22 + 2 * h
    def softmax_at(h): return scores_at(h) + 1
    def exp_at(h): return scores_at(h) + 2
    def normalise_at(h): return scores_at(h) + 3
    def transpose_at(h): return scores_at(h) + 4
    def evacuate_at(h): return scores_at(h) + 5
    def attend_at(h): return scores_at(h) + 6

    def head_at(step_of, s):
        return next((h for h in range(HEADS) if step_of(h) == s), None)

    SCALE = HEAD_DIM ** -0.5
    MASKED = -3.0e38

    ctx = ExitStack()
    with ctx:
        def sb(name, shape, dt=fp32):
            return ctx.enter_context(nc.sbuf_tensor(name, shape, dt))

        def sem(name):
            return ctx.enter_context(nc.semaphore(name))

        w_raw = sb("w_raw", [P, RAW, CHUNK])
        w_hi = sb("w_hi", [P, SPLIT, CHUNK], fp32r)
        w_lo = sb("w_lo", [P, SPLIT, CHUNK], fp32r)
        xt = sb("xt", [P, KT, SEQ])
        x_hi = sb("x_hi", [P, KT, SEQ], fp32r)
        x_lo = sb("x_lo", [P, KT, SEQ], fp32r)
        gain_col = sb("gain_col", [P, KT])
        res = sb("res", [P, TT, D])
        table = sb("table", [P, 2, SEQ])
        edge_recip = sb("edge_recip", [P, GROUPS, EDGE])
        ident = sb("ident", [P, P])
        ones = sb("ones", [P, P])
        mask = sb("mask", [P, 2 * P])
        neg_half = sb("neg_half", [P, TT])
        warm = sb("warm", [P, TT])
        wp = sb("wp", [P, GROUPS, P])
        b_col = sb("b_col", [P, GROUPS])
        scale_col = sb("scale_col", [P, GROUPS])
        final_row = sb("final_row", [P, D])
        square_sum = sb("square_sum", [P, TT])
        mean_square = sb("mean_square", [P, TT])
        rstd = sb("rstd", [P, TT])
        rstd_diag = sb("rstd_diag", [P, SEQ])
        rstd_row = sb("rstd_row", [P, SEQ])
        rope_scaled = sb("rope_scaled", [P, 2, SEQ])
        rope_cos = sb("rope_cos", [P, 2, SEQ])
        rope_sin = sb("rope_sin", [P, 2, SEQ])
        roped = sb("roped", [P, 4, 2, SEQ])
        qk = sb("qk", [P, 2, HEADS // 2, SEQ])
        v = sb("v", [P, TT, WIDTH])
        BLK = 3 * P
        PROBS, PROBS_T = 3, 2
        probs = sb("probs", [P, PROBS, BLK])
        neg_max = sb("neg_max", [P, HEADS, TT])
        denom = sb("denom", [P, HEADS, TT])
        denom_recip = sb("denom_recip", [P, HEADS, TT])
        probs_t = sb("probs_t", [P, PROBS_T, BLK])
        attn = sb("attn", [P, GROUPS, SEQ])
        gate = sb("gate", [P, GROUPS, SEQ])
        sigm = sb("sigm", [P, GROUPS, SEQ])
        PAD = EDGE
        u_pad = sb("u_pad", [P, GROUPS, PAD + SEQ])
        sum_a = sb("sum_a", [P, GROUPS, PAD + SEQ])
        sum_b = sb("sum_b", [P, GROUPS, PAD + SEQ])
        edge_mean = sb("edge_mean", [P, GROUPS, EDGE])
        pooled = sb("pooled", [P, GROUPS, SEQ])
        mixed = sb("mixed", [P, KT, SEQ])
        mixed_hi = sb("mixed_hi", [P, KT, SEQ], fp32r)
        mixed_lo = sb("mixed_lo", [P, KT, SEQ], fp32r)
        out_square = sb("out_square", [P, TT, 2])
        out_mean = sb("out_mean", [P, TT])
        out_rstd = sb("out_rstd", [P, TT])

        bank = [ctx.enter_context(nc.psum_tensor(f"bank{i}", [P, 512], fp32)) for i in range(8)]
        BLOCK_BANKS = [(0, 1), (2, 3)]
        SCORES_BANK, PT_BANK, PV_BANK = (4, 5), 6, 7
        OUT_BANKS = [(0, 1), (4, 5)]
        POOL_BANKS = (6, 7)

        raw_loaded = [sem(f"raw_loaded{i}") for i in range(RAW)]
        first_half_loaded = sem("first_half_loaded")
        xt_loaded = [sem(f"xt_loaded{i}") for i in range(3)]
        gain_loaded = sem("gain_loaded")
        table_loaded = sem("table_loaded")
        res_loaded = [sem(f"res_loaded{i}") for i in range(TT)]
        pool_consts_loaded = sem("pool_consts_loaded")
        final_loaded = sem("final_loaded")
        qk_moved = [sem(f"qk_moved{i}") for i in range(4)]
        x_hi_done, x_lo_done = sem("x_hi_done"), sem("x_lo_done")
        w_hi_done, w_lo_done = sem("w_hi_done"), sem("w_lo_done")
        chunk_used = sem("chunk_used")
        memset_done, consts_done = sem("memset_done"), sem("consts_done")
        square_done, mean_done, rstd_done = sem("square_done"), sem("mean_done"), sem("rstd_done")
        diag_done, bcast_done, rstd_row_done = sem("diag_done"), sem("bcast_done"), sem("rstd_row_done")
        tables_done = sem("tables_done")
        products_done, roped_done = sem("products_done"), sem("roped_done")
        v_done = sem("v_done")
        scores_done, masked_done, exp_done = sem("scores_done"), sem("masked_done"), sem("exp_done")
        recip_done, norm_done = sem("recip_done"), sem("norm_done")
        pt_done, pt_read, pv_done, pv_read = sem("pt_done"), sem("pt_read"), sem("pv_done"), sem("pv_read")
        u_done, sums_done, edge_done, pooled_done = sem("u_done"), sem("sums_done"), sem("edge_done"), sem("pooled_done")
        wpool_done, y_done = sem("wpool_done"), sem("y_done")
        gate_done, sigm_done, gated_done = sem("gate_done"), sem("sigm_done"), sem("gated_done")
        mixed_done, mixed_hi_done, mixed_lo_done = sem("mixed_done"), sem("mixed_hi_done"), sem("mixed_lo_done")
        out_done, added_done, out_square_done = sem("out_done"), sem("added_done"), sem("out_square_done")
        out_mean_done, out_rstd_done = sem("out_mean_done"), sem("out_rstd_done")
        gained_done, scaled_done = sem("gained_done"), sem("scaled_done")
        scaled_dve_done = sem("scaled_dve_done")
        stored = sem("stored")

        def splits(c, slice_=1):
            return c + 1 + slice_ if c == 0 else c + 2

        def chunks_to(place):
            return PER_BLOCK * (place + 1)

        def halves(tile):
            return tile.rearrange("p (s n) -> p s n", s=2)

        block = ctx.enter_context(nc.Block())

        @block.sync
        def _(sp):
            def load_chunk(c):
                slot = w_raw[:, c % RAW, :]
                if c >= RAW:
                    sp.wait_ge(w_lo_done, splits(c - RAW))
                if c < IN_CHUNKS:
                    b, j = ORDER[c // PER_BLOCK], c % PER_BLOCK
                    rows = w_in[2 * j * P:2 * (j + 1) * P, b * WIDTH:(b + 1) * WIDTH]
                    src, dst = rows.rearrange("(s p) n -> p s n", p=P), halves(slot)
                    if c == 0:
                        sp.dma_start(dst[:, 0, :], src[:, 0, :]).then_inc(first_half_loaded, 16)
                        src, dst = src[:, 1, :], dst[:, 1, :]
                else:
                    src, dst = w_out[(c - IN_CHUNKS) * P:(c - IN_CHUNKS + 1) * P, :], slot
                return sp.dma_start(dst, src).then_inc(raw_loaded[c % RAW], 16)

            def load_res(t):
                sp.dma_start(res[:, t, :], x[t * P:(t + 1) * P, :]).then_inc(res_loaded[t], 16)

            x_t_v = x_t.rearrange("(k p) n -> p k n", p=P)
            sp.dma_start(xt[:, 0, :], x_t_v[:, 0, :]).then_inc(xt_loaded[0], 16)
            load_chunk(0)
            sp.dma_start(xt[:, 1:4, :], x_t_v[:, 1:4, :]).then_inc(xt_loaded[1], 16)
            load_chunk(1)
            sp.dma_start(xt[:, 4:KT, :], x_t_v[:, 4:KT, :]).then_inc(xt_loaded[2], 16)
            load_chunk(2)
            load_chunk(3)
            load_res(0)
            load_chunk(4)
            load_chunk(5)
            load_res(1)
            sp.dma_start(table[:, :, :], rope_table).then_inc(table_loaded, 16)

            def move_heads(n):
                sp.wait_ge(roped_done, n + 1)
                for pair in range(2):
                    for f in range(2):
                        sp.dma_start(qk[f:P:2, n // 2, 2 * (n % 2) + pair, :],
                                     roped[HEAD_DIM * pair:HEAD_DIM * (pair + 1), n, f, :]).then_inc(qk_moved[n], 16)

            for c in range(6, CHUNKS):
                if c in (17, 18, 19):
                    move_heads(c - 17)
                if c == 19:
                    move_heads(3)
                load_chunk(c)
                if c == 12:
                    sp.dma_start(wp[:, :, :], w_pool.rearrange("g c d -> c g d")).then_inc(pool_consts_loaded, 16)
                    sp.dma_start(b_col[:, :], b_pool).then_inc(pool_consts_loaded, 16)
                    sp.dma_start(scale_col[:, :], pool_scale).then_inc(pool_consts_loaded, 16)
                    sp.dma_start(edge_recip[:, :, :], edge_table).then_inc(pool_consts_loaded, 16)
                    sp.dma_start(final_row[:, :], final_gain.partition_broadcast(P)).then_inc(final_loaded, 16)
            for t in range(TT):
                sp.wait_ge(scaled_dve_done, t + 1)
                sp.dma_start(out[t * P:(t + 1) * P, 512:], res[:, t, 512:]).then_inc(stored, 16)
            sp.wait_ge(stored, 16 * TT * 2)

        @block.gpsimd
        def _(pool):
            pool.memset(ones[:, :], 1.0).then_inc(memset_done, 1)
            pool.memset(ident[:, :], 0.0).then_inc(memset_done, 1)
            pool.memset(mask[:, :], 0.0).then_inc(memset_done, 1)
            pool.memset(neg_half[:, :], -0.5).then_inc(memset_done, 1)
            pool.memset(u_pad[:, :, 0:PAD], 0.0).then_inc(memset_done, 1)
            pool.wait_ge(memset_done, 5)
            pool.affine_select(out=ident[:, :], in_=ident[:, :], compare_op=ALU.not_equal, fill=1.0,
                               base=0, pattern=[[-1, P]], channel_multiplier=1).then_inc(consts_done, 1)
            pool.affine_select(out=mask[:, P:2 * P], in_=mask[:, P:2 * P], compare_op=ALU.is_ge,
                               fill=MASKED, base=0, pattern=[[-1, P]],
                               channel_multiplier=1).then_inc(consts_done, 1)

            pool.wait_ge(square_done, TT)
            pool.tensor_scalar(mean_square[:, :], square_sum[:, :], EPS, None,
                               ALU.add).then_inc(mean_done, 1)
            pool.wait_ge(mean_done, 1)
            pool.tensor_tensor(rstd[:, :], mean_square[:, :], neg_half[:, :],
                               ALU.pow).then_inc(rstd_done, 1)

            for t in range(TT):
                pool.wait_ge(out_mean_done, t + 1)
                pool.tensor_tensor(out_rstd[:, t:t + 1], out_mean[:, t:t + 1], neg_half[:, 0:1],
                                   ALU.pow).then_inc(out_rstd_done, 1)

        @block.scalar
        def _(act):
            def split_hi(c, slice_=None):
                if slice_ == 0:
                    act.wait_ge(first_half_loaded, 16)
                else:
                    act.wait_ge(raw_loaded[c % RAW], 16 * (c // RAW + 1))
                if c >= SPLIT:
                    act.wait_ge(chunk_used, c - SPLIT + 1)
                part = slice(None) if slice_ is None else slice(slice_ * WIDTH, (slice_ + 1) * WIDTH)
                act.activation(w_hi[:, c % SPLIT, part], w_raw[:, c % RAW, part],
                               ACT.Copy).then_inc(w_hi_done, 1)

            def split_x_hi(k):
                act.wait_ge(xt_loaded[0 if k == 0 else 1 if k < 4 else 2], 16)
                act.activation(x_hi[:, k, :], xt[:, k, :], ACT.Copy,
                               scale=gain_col[:, k:k + 1]).then_inc(x_hi_done, 1)

            def squares(t):
                act.wait_ge(res_loaded[t], 16)
                act.activation(mixed[:, 4 * t:4 * t + 4, :], res[:, t, :].rearrange("p (k n) -> p k n", k=4),
                               ACT.Square, scale=D ** -0.5, accum_out=square_sum[:, t:t + 1]).then_inc(square_done, 1)

            def exps(h):
                act.wait_ge(masked_done, TT * (h + 1))
                for t in range(TT):
                    cols = slice(0, P) if t == 0 else slice(P, BLK)
                    act.activation(probs[:, h % PROBS, cols], probs[:, h % PROBS, cols], ACT.Exp,
                                   bias=neg_max[:, h, t:t + 1], scale=-1.0,
                                   accum_out=denom[:, h, t:t + 1]).then_inc(exp_done, 1)

            def read_probs_t(h):
                act.wait_ge(pt_done, h + 1)
                if h >= PROBS_T:
                    act.wait_ge(pv_done, h - PROBS_T + 1)
                act.activation(probs_t[:, h % PROBS_T, :], bank[PT_BANK][:, 0:BLK],
                               ACT.Copy).then_inc(pt_read, 1)

            def read_v():
                act.wait_ge(chunk_used, chunks_to(V))
                act.wait_ge(rstd_done, 1)
                for t in range(TT):
                    act.activation(v[:, t, :], bank[BLOCK_BANKS[V % 2][t]][:, :], ACT.Copy,
                                   scale=rstd[:, t:t + 1]).then_inc(v_done, 1)

            def read_attn(pair):
                act.wait_ge(pv_done, 2 * pair + 2)
                act.activation(attn[:, pair, :], bank[PV_BANK][:, 0:SEQ], ACT.Copy).then_inc(pv_read, 1)

            def sigmoids(n):
                act.wait_ge(gate_done, 2 * (n + 1))
                if n > 0:
                    act.wait_ge(gated_done, n)
                act.activation(sigm[:, :, :], gate[:, :, :], ACT.Sigmoid).then_inc(sigm_done, 1)

            def split_mixed_hi(k):
                act.wait_ge(mixed_done, k + 1)
                act.activation(mixed_hi[:, k, :], mixed[:, k, :], ACT.Copy).then_inc(mixed_hi_done, 1)

            act.dma_start(gain_col[:, :], gain).then_inc(gain_loaded, 16)
            act.wait_ge(memset_done, 5)
            act.activation(warm[:, :], neg_half[:, :], ACT.Exp)
            act.wait_ge(gain_loaded, 16)
            split_x_hi(0)
            split_hi(0, 0)
            split_x_hi(1)
            split_hi(0, 1)
            split_x_hi(2)
            split_x_hi(3)
            split_hi(1)
            split_x_hi(4)
            split_x_hi(5)
            split_hi(2)
            split_x_hi(6)
            split_x_hi(7)
            split_hi(3)
            for s in range(2, STEPS):
                if s % 2 == 0 and (c := (s + AHEAD) // 2) < CHUNKS:
                    split_hi(c)
                if s == 4:
                    squares(0)
                    squares(1)
                if s == 24:
                    read_v()
                if (h := head_at(exp_at, s)) is not None:
                    exps(h)
                if (h := head_at(evacuate_at, s)) is not None:
                    read_probs_t(h)
                if (h := head_at(attend_at, s - 1)) is not None and h % 2 == 1:
                    read_attn(h // 2)
                if s == 41:
                    sigmoids(0)
                if s == 44:
                    for k in range(GROUPS):
                        split_mixed_hi(k)
                if s == 49:
                    sigmoids(1)
                if s == 51:
                    for k in range(GROUPS, KT):
                        split_mixed_hi(k)

            for t in range(TT):
                for n in range(2):
                    cols = slice(n * 512, (n + 1) * 512)
                    act.wait_ge(added_done, 2 * t + n + 1)
                    act.activation(mixed[:, 4 * t + 2 * n:4 * t + 2 * n + 2, :],
                                   res[:, t, cols].rearrange("p (k n) -> p k n", k=2), ACT.Square, scale=D ** -0.5,
                                   accum_out=out_square[:, t, n:n + 1]).then_inc(out_square_done, 1)
                act.wait_ge(out_rstd_done, t + 1)
                act.wait_ge(gained_done, 2 * t + 1)
                act.activation(res[:, t, 0:512], res[:, t, 0:512], ACT.Copy,
                               scale=out_rstd[:, t:t + 1]).then_inc(scaled_done, 1)
                act.wait_ge(scaled_done, t + 1)
                act.dma_start(out[t * P:(t + 1) * P, 0:512], res[:, t, 0:512]).then_inc(stored, 16)

        @block.vector
        def _(dve):
            def split_lo(c, slice_=None):
                dve.wait_ge(w_hi_done, splits(c) if slice_ is None else splits(c, slice_))
                if c >= SPLIT:
                    dve.wait_ge(chunk_used, c - SPLIT + 1)
                part = slice(None) if slice_ is None else slice(slice_ * WIDTH, (slice_ + 1) * WIDTH)
                dve.tensor_tensor(w_lo[:, c % SPLIT, part], w_raw[:, c % RAW, part],
                                  w_hi[:, c % SPLIT, part].bitcast(fp32),
                                  ALU.subtract).then_inc(w_lo_done, 1)

            def split_x_lo(k):
                dve.wait_ge(x_hi_done, k + 1)
                dve.scalar_tensor_tensor(x_lo[:, k, :], xt[:, k, :], gain_col[:, k:k + 1],
                                         x_hi[:, k, :].bitcast(fp32), ALU.mult,
                                         ALU.subtract).then_inc(x_lo_done, 1)

            def make_diag():
                dve.wait_ge(rstd_done, 1)
                dve.wait_ge(consts_done, 2)
                for t in range(TT):
                    dve.tensor_scalar(rstd_diag[:, t * P:(t + 1) * P], ident[:, :], rstd[:, t:t + 1],
                                      None, ALU.mult).then_inc(diag_done, 1)

            def make_tables():
                dve.wait_ge(bcast_done, 1)
                dve.tensor_copy(rstd_row[:, :], bank[PV_BANK][:, 0:SEQ]).then_inc(rstd_row_done, 1)
                dve.wait_ge(rstd_row_done, 1)
                dve.wait_ge(table_loaded, 16)
                dve.tensor_tensor(rope_scaled[:, :, :], table[:, :, :], over(rstd_row, 2),
                                  ALU.mult).then_inc(tables_done, 1)

            def over(row, n):
                return row[:, :].unsqueeze(1).broadcast_to([P, n, SEQ])

            def rotate(n):
                b = BLOCK_BANKS[(n // 2) % 2][n % 2]
                src = bank[b][:, :].rearrange("p (f n) -> p f n", f=2)
                dve.wait_ge(chunk_used, chunks_to(n // 2))
                dve.wait_ge(tables_done, 1)
                if n > 0:
                    dve.wait_ge(roped_done, n)
                dve.tensor_tensor(rope_cos[:, :, :], src, rope_scaled[:, 0:1, :].broadcast_to([P, 2, SEQ]),
                                  ALU.mult).then_inc(products_done, 1)
                last = dve.tensor_tensor(rope_sin[:, :, :], src,
                                         rope_scaled[:, 1:2, :].broadcast_to([P, 2, SEQ]), ALU.mult)
                last.then_inc(products_done, 1)
                dve.wait_ge(products_done, 2 * (n + 1))
                dve.tensor_tensor(roped[:, n, 0, :], rope_cos[:, 0, :], rope_sin[:, 1, :], ALU.subtract)
                dve.tensor_tensor(roped[:, n, 1, :], rope_cos[:, 1, :], rope_sin[:, 0, :],
                                  ALU.add).then_inc(roped_done, 1)

            def mask_and_max(h):
                dve.wait_ge(scores_done, h + 1)
                if h >= PROBS:
                    dve.wait_ge(pt_done, h - PROBS + 1)
                b = bank[SCORES_BANK[h % 2]]
                for t in range(TT):
                    cols, m = (slice(0, P), slice(P, 2 * P)) if t == 0 else (slice(P, BLK), slice(0, 2 * P))
                    dve.tensor_tensor_reduce(out=probs[:, h % PROBS, cols], in0=b[:, cols], in1=mask[:, m],
                                             scale=-SCALE, scalar=-MASKED, op0=ALU.add, op1=ALU.min,
                                             accum_out=neg_max[:, h, t:t + 1]).then_inc(masked_done, 1)

            def normalise(h):
                dve.wait_ge(exp_done, TT * (h + 1))
                dve.reciprocal(denom_recip[:, h, :], denom[:, h, :]).then_inc(recip_done, 1)
                dve.wait_ge(recip_done, h + 1)
                for t in range(TT):
                    cols = slice(0, P) if t == 0 else slice(P, BLK)
                    dve.tensor_scalar(probs[:, h % PROBS, cols], probs[:, h % PROBS, cols],
                                      denom_recip[:, h, t:t + 1], None, ALU.mult).then_inc(norm_done, 1)

            def read_rows(place, dst, done):
                dve.wait_ge(chunk_used, chunks_to(place))
                for i, b in enumerate(BLOCK_BANKS[place % 2]):
                    dve.tensor_tensor(dst[:, 2 * i:2 * i + 2, :],
                                      bank[b][:, :].rearrange("p (f n) -> p f n", f=2), over(rstd_row, 2),
                                      ALU.mult).then_inc(done, 1)

            sums = (sum_a, sum_b)

            def double(g):
                src, dst, shift = (u_pad if g == 0 else sums[(g - 1) % 2]), sums[g % 2], 1 << g
                lo = 2 * shift - 1
                dve.wait_ge(u_done, 2)
                if g > 0:
                    dve.wait_ge(sums_done, g)
                dve.tensor_tensor(dst[:, g:GROUPS, lo:], src[:, g:GROUPS, lo:],
                                  src[:, g:GROUPS, lo - shift:PAD + SEQ - shift],
                                  ALU.add).then_inc(sums_done, 1)

            def pool_minus_token(g):
                dve.wait_ge(sums_done, GROUPS)
                dve.wait_ge(pool_consts_loaded, 16 * 4)
                s = sums[g % 2]
                dve.tensor_tensor(edge_mean[:, g, :], s[:, g, PAD:PAD + EDGE], edge_recip[:, g, :],
                                  ALU.mult).then_inc(edge_done, 1)
                dve.scalar_tensor_tensor(pooled[:, g, EDGE:], s[:, g, PAD + EDGE:], 1.0 / WINDOWS[g],
                                         u_pad[:, g, PAD + EDGE:], ALU.mult,
                                         ALU.subtract).then_inc(pooled_done, 1)
                dve.wait_ge(edge_done, g + 1)
                dve.tensor_tensor(pooled[:, g, 0:EDGE], edge_mean[:, g, :], u_pad[:, g, PAD:PAD + EDGE],
                                  ALU.subtract).then_inc(pooled_done, 1)

            def bias_and_scale(i):
                dve.wait_ge(wpool_done, i + 1)
                for g in (2 * i, 2 * i + 1):
                    dve.tensor_scalar(pooled[:, g, :], bank[POOL_BANKS[i]][:, (g % 2) * SEQ:(g % 2 + 1) * SEQ],
                                      b_col[:, g:g + 1], scale_col[:, g:g + 1], ALU.add,
                                      ALU.mult).then_inc(y_done, 1)

            def gate_silu(n):
                dve.wait_ge(sigm_done, n + 1)
                dve.tensor_tensor(gate[:, :, :], gate[:, :, :], sigm[:, :, :],
                                  ALU.mult).then_inc(gated_done, 1)

            def mix(k):
                g, n = k % GROUPS, k // GROUPS
                dve.wait_ge(gated_done, n + 1)
                if n == 0:
                    dve.wait_ge(pv_read, g + 1)
                else:
                    dve.wait_ge(y_done, g + 1)
                dve.tensor_tensor(mixed[:, k, :], (attn if n == 0 else pooled)[:, g, :], gate[:, g, :],
                                  ALU.mult).then_inc(mixed_done, 1)

            def split_mixed_lo(k):
                dve.wait_ge(mixed_hi_done, k + 1)
                dve.tensor_tensor(mixed_lo[:, k, :], mixed[:, k, :], mixed_hi[:, k, :].bitcast(fp32),
                                  ALU.subtract).then_inc(mixed_lo_done, 1)

            dve.wait_ge(gain_loaded, 16)
            split_x_lo(0)
            split_lo(0, 0)
            split_x_lo(1)
            split_lo(0, 1)
            split_x_lo(2)
            split_x_lo(3)
            split_lo(1)
            split_x_lo(4)
            split_x_lo(5)
            split_lo(2)
            split_x_lo(6)
            split_x_lo(7)
            split_lo(3)
            for s in range(2, STEPS):
                if s == 6:
                    make_diag()
                if s % 2 == 0 and (c := (s + AHEAD) // 2) < CHUNKS:
                    split_lo(c)
                if s == 9:
                    make_tables()
                if s in (10, 12, 16, 17):
                    rotate((10, 12, 16, 17).index(s))
                if (h := head_at(softmax_at, s)) is not None:
                    mask_and_max(h)
                if (h := head_at(normalise_at, s)) is not None:
                    normalise(h)
                if s == 32:
                    read_rows(U, u_pad[:, :, PAD:], u_done)
                if s in (33, 34, 35, 36):
                    double(s - 33)
                if s in (37, 38, 39, 40):
                    pool_minus_token(s - 37)
                if s == 40:
                    read_rows(GA, gate, gate_done)
                if s == 42:
                    gate_silu(0)
                if s == 44:
                    for k in range(GROUPS):
                        mix(k)
                        if k > 0:
                            split_mixed_lo(k - 1)
                    split_mixed_lo(GROUPS - 1)
                if s == 46:
                    bias_and_scale(0)
                    bias_and_scale(1)
                if s == 48:
                    dve.wait_ge(mixed_done, GROUPS)
                    read_rows(GP, gate, gate_done)
                if s == 50:
                    gate_silu(1)
                if s == 51:
                    for k in range(GROUPS, KT):
                        mix(k)
                        if k > GROUPS:
                            split_mixed_lo(k - 1)
                    split_mixed_lo(KT - 1)

            for t in range(TT):
                for n in range(2):
                    cols = slice(n * 512, (n + 1) * 512)
                    dve.wait_ge(out_done, 2 * t + n + 1)
                    dve.tensor_tensor(res[:, t, cols], bank[OUT_BANKS[t][n]][:, :], res[:, t, cols],
                                      ALU.add).then_inc(added_done, 1)
                dve.wait_ge(out_square_done, 2 * (t + 1))
                dve.tensor_scalar(out_mean[:, t:t + 1], out_square[:, t, 0:1], out_square[:, t, 1:2], EPS,
                                  ALU.add, ALU.add).then_inc(out_mean_done, 1)
                dve.wait_ge(final_loaded, 16)
                for n in range(2):
                    cols = slice(n * 512, (n + 1) * 512)
                    dve.tensor_tensor(res[:, t, cols], res[:, t, cols], final_row[:, cols],
                                      ALU.mult).then_inc(gained_done, 1)
                dve.wait_ge(gained_done, 2 * (t + 1))
                dve.wait_ge(out_rstd_done, t + 1)
                dve.tensor_scalar(res[:, t, 512:], res[:, t, 512:], out_rstd[:, t:t + 1], None,
                                  ALU.mult).then_inc(scaled_dve_done, 1)

        @block.tensor
        def _(pe):
            PASSES = ((w_hi, 0), (w_hi, 1), (w_lo, 0))

            def wait_for_split(c, slice_, lo):
                if c == 0 or slice_ == 0:
                    pe.wait_ge(w_lo_done if lo else w_hi_done, splits(c, slice_))

            def wait_for_banks(place):
                if place == V:
                    pe.wait_ge(products_done, 4)
                if place == U:
                    pe.wait_ge(products_done, 8)
                if place == GA:
                    pe.wait_ge(v_done, TT)
                if place == GP:
                    pe.wait_ge(u_done, 2)

            def project(s):
                place, k, c = s // KT, s % KT, s // 2
                if k == 0:
                    wait_for_banks(place)
                for n, (w, lo) in enumerate(PASSES):
                    if n != 1:
                        wait_for_split(c, s % 2, lo=(n == 2))
                    if place == Q and n < 2:
                        pe.wait_ge((x_hi_done, x_lo_done)[n], k + 1)
                    act, tile = (x_hi, x_lo)[lo], halves(w[:, c % SPLIT, :])[:, k % 2, :]
                    first, last = k == 0 and n == 0, k == KT - 1 and n == 2
                    if place == V:
                        for t in range(TT):
                            mm = pe.matmul(bank[BLOCK_BANKS[0][t]][:, :], act[:, k, t * P:(t + 1) * P], tile,
                                           start=first, stop=last, skip_group_check=True)
                        continue
                    for i in range(4):
                        cols = tile[:, i * P:(i + 1) * P]
                        mm = pe.matmul(bank[BLOCK_BANKS[place % 2][i // 2]][:, (i % 2) * SEQ:(i % 2 + 1) * SEQ],
                                       cols, act[:, k, :], start=first and i % 2 == 0, stop=last,
                                       skip_group_check=True)
                return mm

            def project_out(k, t):
                c = IN_CHUNKS + k
                for n, (w, lo) in enumerate(PASSES):
                    if n != 1:
                        pe.wait_ge(w_lo_done if n == 2 else w_hi_done, splits(c))
                    if n < 2:
                        pe.wait_ge((mixed_hi_done, mixed_lo_done)[n], k + 1)
                    act = (mixed_hi, mixed_lo)[lo]
                    for h in range(2):
                        cols = slice(h * 512, (h + 1) * 512)
                        mm = pe.matmul(bank[OUT_BANKS[t][h]][:, :], act[:, k, t * P:(t + 1) * P],
                                       w[:, c % SPLIT, cols], start=(k == 0 and n == 0),
                                       stop=(k == KT - 1 and n == 2), skip_group_check=True)
                        if k == KT - 1 and n == 2:
                            mm.then_inc(out_done, 1)
                return mm

            def scores(h):
                n, at = h // 4, HEAD_DIM * (h % 2)
                pe.wait_ge(qk_moved[n], 16 * 4)
                pe.wait_ge(qk_moved[2 + n], 16 * 4)
                if h >= 2:
                    pe.wait_ge(masked_done, TT * (h - 1))
                b = bank[SCORES_BANK[h % 2]]
                q_h, k_h = (qk[at:at + HEAD_DIM, i, h // 2, :] for i in range(2))
                pe.matmul(b[:, 0:P], q_h[:, 0:P], k_h[:, 0:P], start=True, stop=True)
                pe.matmul(b[:, P:BLK], q_h[:, P:SEQ], k_h, start=True,
                          stop=True).then_inc(scores_done, 1)

            def transpose(h):
                pe.wait_ge(norm_done, TT * (h + 1))
                pe.wait_ge(pt_read, h) if h > 0 else None
                for i in range(3):
                    mm = pe.transpose(bank[PT_BANK][:, i * P:(i + 1) * P],
                                      probs[:, h % PROBS, i * P:(i + 1) * P], ident[:, :])
                mm.then_inc(pt_done, 1)

            def attend(h):
                at = HEAD_DIM * (h % 2)
                pe.wait_ge(v_done, TT)
                pe.wait_ge(pt_read, h + 1)
                if h >= 2:
                    pe.wait_ge(pv_read, h // 2)
                o, pt = bank[PV_BANK][at:at + HEAD_DIM, :], probs_t[:, h % PROBS_T, :]
                v_h = v[:, :, h * HEAD_DIM:(h + 1) * HEAD_DIM]
                pe.matmul(o[:, 0:SEQ], v_h[:, 0, :], pt[:, 0:SEQ], start=True, stop=False)
                pe.matmul(o[:, P:SEQ], v_h[:, 1, :], pt[:, SEQ:BLK], start=False,
                          stop=True).then_inc(pv_done, 1)

            def broadcast_rstd():
                for t in range(TT):
                    pe.wait_ge(diag_done, t + 1)
                    mm = pe.matmul(bank[PV_BANK][:, t * P:(t + 1) * P], ones[:, :],
                                   rstd_diag[:, t * P:(t + 1) * P], start=True, stop=True)
                mm.then_inc(bcast_done, 1)

            def pool_weights(i):
                pe.wait_ge(pt_read, HEADS)
                pe.wait_ge(pv_read, HEADS // 2)
                pe.wait_ge(pool_consts_loaded, 16 * 4)
                for g in (2 * i, 2 * i + 1):
                    pe.wait_ge(pooled_done, 2 * (g + 1))
                    mm = pe.matmul(bank[POOL_BANKS[i]][:, (g % 2) * SEQ:(g % 2 + 1) * SEQ], wp[:, g, :],
                                   pooled[:, g, :], start=True, stop=True)
                mm.then_inc(wpool_done, 1)

            pe.wait_ge(consts_done, 2)
            for _ in range(WARM_UP):
                pe.matmul(bank[PT_BANK][:, 0:P], ones[:, :], ident[:, :], start=True, stop=True)
            for s in range(OUT_STEP):
                mm = project(s)
                if s % 2 == 1:
                    mm.then_inc(chunk_used, 1)
                if s == 10:
                    broadcast_rstd()
                if (h := head_at(scores_at, s)) is not None:
                    scores(h)
                if (h := head_at(transpose_at, s)) is not None:
                    transpose(h)
                if (h := head_at(attend_at, s)) is not None:
                    attend(h)
                if s in (44, 45):
                    pool_weights(s - 44)
            pe.wait_ge(gate_done, 2)
            for k in range(KT - 2):
                project_out(k, 0)
                project_out(k, 1).then_inc(chunk_used, 1)
            for t in range(TT):
                for k in range(KT - 2, KT):
                    project_out(k, t)


def kernel(**inputs):
    import concourse.bacc as bacc
    from concourse.bass_utils import run_bass_kernel_spmd

    inputs = {name: np.asarray(a) for name, a in inputs.items()}
    x = np.ascontiguousarray(inputs["x"])[0]
    arrays = {
        "x": x,
        "x_t": np.ascontiguousarray(x.T),
        "gain": np.ascontiguousarray(inputs["norm_gain"][0].reshape(KT, P).T),
        "w_in": rotary_columns_together(inputs["w_in"][0]),
        "w_pool": np.ascontiguousarray(inputs["w_pool"][0]),
        "b_pool": np.ascontiguousarray(inputs["b_pool"][0].T),
        "pool_scale": np.ascontiguousarray(inputs["pool_scale"][0].reshape(GROUPS, P).T),
        "w_out": np.ascontiguousarray(inputs["w_out"][0]),
        "final_gain": np.ascontiguousarray(inputs["final_gain"]),
        "rope_table": rope_constants(),
        "edge_table": edge_constants(),
    }
    nc = bacc.Bacc("TRN2", target_bir_lowering=False, num_devices=1)
    args = [nc.dram_tensor("in_" + name, a.shape, mybir.dt.from_np(a.dtype), kind="ExternalInput").ap()
            for name, a in arrays.items()]
    out = nc.dram_tensor("out_dram", (SEQ, D), mybir.dt.float32, kind="ExternalOutput").ap()
    hymba_kernel(nc, *args, out)
    r = run_bass_kernel_spmd(nc, [{"in_" + name: a for name, a in arrays.items()}], core_ids=[0])
    return r.results[0]["out_dram"].reshape(1, SEQ, D)


def rotary_columns_together(w_in):
    qk = w_in[:, :2 * WIDTH].reshape(D, 2, 2, 4, 2, HALF).transpose(0, 1, 2, 4, 3, 5)
    return np.ascontiguousarray(np.concatenate([qk.reshape(D, 2 * WIDTH), w_in[:, 2 * WIDTH:]], axis=1))


def rope_constants():
    inv_freq = (np.float32(1.0) / np.float32(THETA) ** (np.arange(0, HEAD_DIM, 2, dtype=np.float32)
                                                        / np.float32(HEAD_DIM))).astype(np.float32)
    angle = inv_freq[:, None] * np.arange(SEQ, dtype=np.float32)[None, :]
    both = np.stack([np.cos(angle), np.sin(angle)], axis=1).astype(np.float32)
    return np.ascontiguousarray(np.tile(both, (P // HALF, 1, 1)))


def edge_constants():
    counts = np.minimum(np.arange(1, EDGE + 1)[None, :], np.array(WINDOWS)[:, None])
    one = (np.float32(1.0) / counts.astype(np.float32)).astype(np.float32)
    return np.ascontiguousarray(np.broadcast_to(one, (P, GROUPS, EDGE)))
```

```python
import concourse.bass as bass
from concourse import mybir
from contextlib import ExitStack

import numpy as np

SEQ, D = 256, 1024
HEADS, HEAD_DIM = 8, 64
WIDTH = HEADS * HEAD_DIM
BLOCKS = 6
WINDOWS = (2, 4, 8, 16)
GROUPS = len(WINDOWS)
EPS = 1e-6
THETA = 10000.0
P = 128
KT = D // P
TT = SEQ // P
HALF = HEAD_DIM // 2
WARM_UP = 9
EDGE = max(WINDOWS)


def hymba_kernel(nc, x, x_t, gain, w_in, w_pool, b_pool, pool_scale, w_out, final_gain,
                 rope_table, edge_table, out):
    fp32, fp32r = mybir.dt.float32, mybir.dt.float32r
    ALU, ACT = mybir.AluOpType, mybir.ActivationFunctionType

    ORDER = [0, 1, 2, 4, 5, 3]
    Q, K, V, U, GP, GA = range(BLOCKS)
    CHUNK = 1024
    PER_BLOCK = KT * WIDTH // CHUNK
    IN_CHUNKS = BLOCKS * PER_BLOCK
    CHUNKS = IN_CHUNKS + KT
    RAW, SPLIT = 8, 5
    STEPS = 2 * CHUNKS
    OUT_STEP = 2 * IN_CHUNKS
    AHEAD = 8

    def scores_at(h): return 25 + 2 * h
    def softmax_at(h): return scores_at(h) + 1
    def exp_at(h): return scores_at(h) + 2
    def normalise_at(h): return scores_at(h) + 3
    def transpose_at(h): return scores_at(h) + 4
    def evacuate_at(h): return scores_at(h) + 5
    def attend_at(h): return scores_at(h) + 6

    ROTATE_AT = (9, 16, 18, 20)

    def head_at(step_of, s):
        return next((h for h in range(HEADS) if step_of(h) == s), None)

    SCALE = HEAD_DIM ** -0.5
    MASKED = -3.0e38

    ctx = ExitStack()
    with ctx:
        def sb(name, shape, dt=fp32):
            return ctx.enter_context(nc.sbuf_tensor(name, shape, dt))

        def sem(name):
            return ctx.enter_context(nc.semaphore(name))

        w_raw = sb("w_raw", [P, RAW, CHUNK])
        w_hi = sb("w_hi", [P, SPLIT, CHUNK], fp32r)
        w_lo = sb("w_lo", [P, SPLIT, CHUNK], fp32r)
        xt = sb("xt", [P, KT, SEQ])
        x_hi = sb("x_hi", [P, KT, SEQ], fp32r)
        x_lo = sb("x_lo", [P, KT, SEQ], fp32r)
        gain_col = sb("gain_col", [P, KT])
        res = sb("res", [P, TT, D])
        table = sb("table", [P, 2, SEQ])
        edge_recip = sb("edge_recip", [P, GROUPS, EDGE])
        ident = sb("ident", [P, P])
        ones = sb("ones", [P, P])
        mask = sb("mask", [P, 2 * P])
        neg_half = sb("neg_half", [P, TT])
        warm = sb("warm", [P, TT])
        wp = sb("wp", [P, GROUPS, P])
        b_col = sb("b_col", [P, GROUPS])
        scale_col = sb("scale_col", [P, GROUPS])
        final_row = sb("final_row", [P, D])
        square_sum = sb("square_sum", [P, TT])
        mean_square = sb("mean_square", [P, TT])
        rstd = sb("rstd", [P, TT])
        rstd_diag = sb("rstd_diag", [P, SEQ])
        rstd_row = sb("rstd_row", [P, SEQ])
        rope_scaled = sb("rope_scaled", [P, 2, SEQ])
        unrotated = sb("unrotated", [P, 4, 2, SEQ])
        roped = sb("roped", [P, 4, 2, SEQ])
        qk = sb("qk", [P, 2, HEADS // 2, SEQ])
        v = sb("v", [P, TT, WIDTH])
        BLK = 3 * P
        PROBS, PROBS_T = 3, 2
        probs = sb("probs", [P, PROBS, BLK])
        neg_max = sb("neg_max", [P, HEADS, TT])
        denom = sb("denom", [P, HEADS, TT])
        denom_recip = sb("denom_recip", [P, HEADS, TT])
        probs_t = sb("probs_t", [P, PROBS_T, BLK])
        attn = sb("attn", [P, GROUPS, SEQ])
        rope_sin = attn[:, 0:2, :]
        gate = sb("gate", [P, GROUPS, SEQ])
        sigm = sb("sigm", [P, GROUPS, SEQ])
        PAD = EDGE
        u_pad = sb("u_pad", [P, GROUPS, PAD + SEQ])
        sum_a = sb("sum_a", [P, GROUPS, PAD + SEQ])
        sum_b = sb("sum_b", [P, GROUPS, PAD + SEQ])
        edge_mean = sb("edge_mean", [P, GROUPS, EDGE])
        pooled = sb("pooled", [P, GROUPS, SEQ])
        mixed = sb("mixed", [P, KT, SEQ])
        mixed_hi = sb("mixed_hi", [P, KT, SEQ], fp32r)
        mixed_lo = sb("mixed_lo", [P, KT, SEQ], fp32r)
        out_square = sb("out_square", [P, TT, 2])
        out_mean = sb("out_mean", [P, TT])
        mean_others = sb("mean_others", [P, 1])
        square_out = [tile[:, :, :].rearrange("p g n -> p (g n)") for tile in (attn, sigm)]
        last_square = gate[:, 0, :]
        gained = mixed[:, :, :].rearrange("p (t k) n -> p t (k n)", t=TT)
        out_rstd = sb("out_rstd", [P, TT])

        bank = [ctx.enter_context(nc.psum_tensor(f"bank{i}", [P, 512], fp32)) for i in range(8)]
        BLOCK_BANKS = [(0, 1), (2, 3)]
        SCORES_BANK, PT_BANK, PV_BANK = (4, 5), 6, 7
        POOL_BANKS = (0, 1)
        OUT_PARTS = (((0, 512, 0), (512, 512, 1)), ((0, 512, 4), (512, 256, 5), (768, 256, 7)))
        TAIL = 4
        SCALED_BY_ACT = 384

        raw_loaded = [sem(f"raw_loaded{i}") for i in range(RAW)]
        FINE = 2
        first_slice_loaded = [sem(f"first_slice_loaded{i}") for i in range(FINE)]
        XT_PARTS = ((0, 1), (1, 2), (2, 4), (4, 6), (6, KT))
        xt_loaded = [sem(f"xt_loaded{i}") for i in range(len(XT_PARTS))]
        gain_loaded = sem("gain_loaded")
        table_loaded = sem("table_loaded")
        res_loaded = [sem(f"res_loaded{i}") for i in range(TT)]
        pool_consts_loaded = sem("pool_consts_loaded")
        final_loaded = sem("final_loaded")
        qk_moved = [sem(f"qk_moved{i}") for i in range(4)]
        x_hi_done, x_lo_done = sem("x_hi_done"), sem("x_lo_done")
        w_hi_done, w_lo_done = sem("w_hi_done"), sem("w_lo_done")
        chunk_used = sem("chunk_used")
        memset_done, consts_done = sem("memset_done"), sem("consts_done")
        square_done, mean_done, rstd_done = sem("square_done"), sem("mean_done"), sem("rstd_done")
        diag_done, bcast_done, rstd_row_done = sem("diag_done"), sem("bcast_done"), sem("rstd_row_done")
        tables_done = sem("tables_done")
        qk_read, products_done, roped_done = sem("qk_read"), sem("products_done"), sem("roped_done")
        v_done = sem("v_done")
        scores_done, masked_done, exp_done = sem("scores_done"), sem("masked_done"), sem("exp_done")
        recip_done, norm_done = sem("recip_done"), sem("norm_done")
        pt_done, pt_read, pv_done, pv_read = sem("pt_done"), sem("pt_read"), sem("pv_done"), sem("pv_read")
        u_done, sums_done, edge_done, pooled_done = sem("u_done"), sem("sums_done"), sem("edge_done"), sem("pooled_done")
        wpool_done, pool_gated = sem("wpool_done"), sem("pool_gated")
        gate_done, sigm_done, attn_gated = sem("gate_done"), sem("sigm_done"), sem("attn_gated")
        mixed_done, mixed_hi_done, mixed_lo_done = sem("mixed_done"), sem("mixed_hi_done"), sem("mixed_lo_done")
        out_done, added_done, out_square_done = sem("out_done"), sem("added_done"), sem("out_square_done")
        out_mean_done, out_rstd_done = sem("out_mean_done"), sem("out_rstd_done")
        gained_done, scaled_done = sem("gained_done"), sem("scaled_done")
        scaled_act_done, mean_others_done = sem("scaled_act_done"), sem("mean_others_done")
        stored = sem("stored")

        def splits(c, slice_=1):
            return 2 * c + slice_ + 1 if c < FINE else c + 1 + FINE

        def chunks_to(place):
            return PER_BLOCK * (place + 1)

        def halves(tile):
            return tile.rearrange("p (s n) -> p s n", s=2)

        block = ctx.enter_context(nc.Block())

        @block.sync
        def _(sp):
            def load_chunk(c, slice_=None):
                slot = w_raw[:, c % RAW, :]
                if c >= RAW:
                    sp.wait_ge(w_lo_done, splits(c - RAW))
                if c < IN_CHUNKS:
                    b, j = ORDER[c // PER_BLOCK], c % PER_BLOCK
                    rows = w_in[2 * j * P:2 * (j + 1) * P, b * WIDTH:(b + 1) * WIDTH]
                    src, dst = rows.rearrange("(s p) n -> p s n", p=P), halves(slot)
                    if slice_ is not None:
                        src, dst = src[:, slice_, :], dst[:, slice_, :]
                else:
                    rows = (c - IN_CHUNKS + GROUPS) % KT
                    src, dst = w_out[rows * P:(rows + 1) * P, :], slot
                sp.dma_start(dst, src).then_inc(first_slice_loaded[c] if slice_ == 0 else raw_loaded[c % RAW], 16)

            def load_res(t):
                sp.dma_start(res[:, t, :], x[t * P:(t + 1) * P, :]).then_inc(res_loaded[t], 16)

            def load_xt(i):
                lo, hi = XT_PARTS[i]
                sp.dma_start(xt[:, lo:hi, :], x_t.rearrange("(k p) n -> p k n", p=P)[:, lo:hi, :]).then_inc(
                    xt_loaded[i], 16)

            load_xt(0)
            load_chunk(0, 0)
            load_xt(1)
            load_chunk(0, 1)
            load_xt(2)
            load_chunk(1, 0)
            load_chunk(1, 1)
            load_xt(3)
            load_chunk(2)
            load_xt(4)
            load_chunk(3)
            load_chunk(4)
            load_res(0)
            load_chunk(5)
            load_res(1)
            load_chunk(6)
            sp.dma_start(table[:, :, :], rope_table).then_inc(table_loaded, 16)

            def move_heads(n):
                sp.wait_ge(roped_done, n + 1)
                for pair in range(2):
                    for f in range(2):
                        sp.dma_start(qk[f:P:2, n % 2, 2 * (n // 2) + pair, :],
                                     roped[HEAD_DIM * pair:HEAD_DIM * (pair + 1), n, f, :]).then_inc(qk_moved[n], 16)

            for c in range(7, CHUNKS):
                if c == 17:
                    move_heads(0)
                    move_heads(1)
                if c in (19, 20):
                    move_heads(c - 17)
                load_chunk(c)
                if c == 21:
                    sp.dma_start(wp[:, :, :], w_pool.rearrange("g c d -> c g d")).then_inc(pool_consts_loaded, 16)
                    sp.dma_start(b_col[:, :], b_pool).then_inc(pool_consts_loaded, 16)
                    sp.dma_start(scale_col[:, :], pool_scale).then_inc(pool_consts_loaded, 16)
                    sp.dma_start(edge_recip[:, :, :], edge_table).then_inc(pool_consts_loaded, 16)
                    sp.dma_start(final_row[:, :], final_gain.partition_broadcast(P)).then_inc(final_loaded, 16)
            sp.wait_ge(scaled_act_done, 1)
            sp.dma_start(out[0:P, :], res[:, 0, :]).then_inc(stored, 16)
            sp.wait_ge(scaled_done, 1)
            sp.dma_start(out[P:, SCALED_BY_ACT:], res[:, 1, SCALED_BY_ACT:]).then_inc(stored, 16)
            sp.wait_ge(stored, 16 * 3)

        @block.gpsimd
        def _(pool):
            pool.memset(ones[:, :], 1.0).then_inc(memset_done, 1)
            pool.memset(ident[:, :], 0.0).then_inc(memset_done, 1)
            pool.memset(mask[:, :], 0.0).then_inc(memset_done, 1)
            pool.memset(neg_half[:, :], -0.5).then_inc(memset_done, 1)
            pool.memset(u_pad[:, :, 0:PAD], 0.0).then_inc(memset_done, 1)
            pool.wait_ge(memset_done, 5)
            pool.affine_select(out=ident[:, :], in_=ident[:, :], compare_op=ALU.not_equal, fill=1.0,
                               base=0, pattern=[[-1, P]], channel_multiplier=1).then_inc(consts_done, 1)
            pool.affine_select(out=mask[:, P:2 * P], in_=mask[:, P:2 * P], compare_op=ALU.is_ge,
                               fill=MASKED, base=0, pattern=[[-1, P]],
                               channel_multiplier=1).then_inc(consts_done, 1)

            pool.wait_ge(square_done, TT)
            pool.tensor_scalar(mean_square[:, :], square_sum[:, :], EPS, None,
                               ALU.add).then_inc(mean_done, 1)
            pool.wait_ge(mean_done, 1)
            pool.tensor_tensor(rstd[:, :], mean_square[:, :], neg_half[:, :],
                               ALU.pow).then_inc(rstd_done, 1)

            for t in range(TT):
                pool.wait_ge(out_mean_done, t + 1)
                pool.tensor_tensor(out_rstd[:, t:t + 1], out_mean[:, t:t + 1], neg_half[:, 0:1],
                                   ALU.pow).then_inc(out_rstd_done, 1)

        @block.scalar
        def _(act):
            def split_hi(c, slice_=None):
                if slice_ == 0:
                    act.wait_ge(first_slice_loaded[c], 16)
                else:
                    act.wait_ge(raw_loaded[c % RAW], 16 * (c // RAW + 1))
                if c >= SPLIT:
                    act.wait_ge(chunk_used, c - SPLIT + 1)
                part = slice(None) if slice_ is None else slice(slice_ * WIDTH, (slice_ + 1) * WIDTH)
                act.activation(w_hi[:, c % SPLIT, part], w_raw[:, c % RAW, part],
                               ACT.Copy).then_inc(w_hi_done, 1)

            def split_x_hi(k):
                act.wait_ge(xt_loaded[next(i for i, (lo, hi) in enumerate(XT_PARTS) if lo <= k < hi)], 16)
                act.activation(x_hi[:, k, :], xt[:, k, :], ACT.Copy,
                               scale=gain_col[:, k:k + 1]).then_inc(x_hi_done, 1)

            def squares(t):
                act.wait_ge(res_loaded[t], 16)
                act.activation(mixed[:, 4 * t:4 * t + 4, :], res[:, t, :].rearrange("p (k n) -> p k n", k=4),
                               ACT.Square, scale=D ** -0.5, accum_out=square_sum[:, t:t + 1]).then_inc(square_done, 1)

            def exps(h):
                act.wait_ge(masked_done, TT * (h + 1))
                for t in range(TT):
                    cols = slice(0, P) if t == 0 else slice(P, BLK)
                    act.activation(probs[:, h % PROBS, cols], probs[:, h % PROBS, cols], ACT.Exp,
                                   bias=neg_max[:, h, t:t + 1], scale=-1.0,
                                   accum_out=denom[:, h, t:t + 1]).then_inc(exp_done, 1)

            def read_probs_t(h):
                act.wait_ge(pt_done, h + 1)
                if h >= PROBS_T:
                    act.wait_ge(pv_done, h - PROBS_T + 1)
                act.activation(probs_t[:, h % PROBS_T, :], bank[PT_BANK][:, 0:BLK],
                               ACT.Copy).then_inc(pt_read, 1)

            def read_qk(n):
                act.wait_ge(chunk_used, chunks_to(n // 2))
                act.activation(unrotated[:, n, :, :], bank[BLOCK_BANKS[n // 2][n % 2]][:, :].rearrange(
                    "p (f n) -> p f n", f=2), ACT.Copy).then_inc(qk_read, 1)

            def read_v():
                act.wait_ge(chunk_used, chunks_to(V))
                act.wait_ge(rstd_done, 1)
                for t in range(TT):
                    act.activation(v[:, t, :], bank[BLOCK_BANKS[V % 2][t]][:, :], ACT.Copy,
                                   scale=rstd[:, t:t + 1]).then_inc(v_done, 1)

            def read_attn(pair):
                act.wait_ge(pv_done, 2 * pair + 2)
                act.activation(attn[:, pair, :], bank[PV_BANK][:, 0:SEQ], ACT.Copy).then_inc(pv_read, 1)

            def sigmoids(n):
                act.wait_ge(gate_done, 2 * (n + 1))
                if n > 0:
                    act.wait_ge(mixed_done, GROUPS)
                act.activation(sigm[:, :, :], gate[:, :, :], ACT.Sigmoid).then_inc(sigm_done, 1)

            def split_mixed_hi(k):
                act.wait_ge(mixed_done, k + 1)
                act.activation(mixed_hi[:, k, :], mixed[:, k, :], ACT.Copy).then_inc(mixed_hi_done, 1)

            act.dma_start(gain_col[:, :], gain).then_inc(gain_loaded, 16)
            act.wait_ge(memset_done, 5)
            act.activation(warm[:, :], neg_half[:, :], ACT.Exp)
            act.wait_ge(gain_loaded, 16)
            split_x_hi(0)
            split_hi(0, 0)
            split_x_hi(1)
            split_hi(0, 1)
            split_x_hi(2)
            split_hi(1, 0)
            split_x_hi(3)
            split_hi(1, 1)
            split_x_hi(4)
            split_x_hi(5)
            split_hi(2)
            split_x_hi(6)
            split_x_hi(7)
            split_hi(3)
            for s in range(STEPS):
                if s in (8, 9, 16, 17):
                    read_qk((8, 9, 16, 17).index(s))
                if s == 24:
                    read_v()
                if (h := head_at(exp_at, s)) is not None:
                    exps(h)
                if (h := head_at(evacuate_at, s)) is not None:
                    read_probs_t(h)
                if (h := head_at(attend_at, s - 1)) is not None and h % 2 == 1:
                    read_attn(h // 2)
                if s == 41:
                    sigmoids(0)
                if s in (45, 52):
                    for k in range(GROUPS) if s == 45 else range(GROUPS, KT):
                        split_mixed_hi(k)
                if s % 2 == 0 and (c := (s + AHEAD) // 2) < CHUNKS:
                    split_hi(c)
                if s == 2:
                    squares(0)
                    squares(1)
                if s == 51:
                    sigmoids(1)

            def squares_of_part(t, i):
                at, size, _ = OUT_PARTS[t][i]
                act.wait_ge(added_done, len(OUT_PARTS[0]) * t + i + 1)
                act.activation(square_out[t][:, at:at + size], res[:, t, at:at + size], ACT.Square,
                               scale=D ** -0.5, accum_out=out_square[:, t, i:i + 1]).then_inc(out_square_done, 1)

            def scale_tile(t, columns):
                act.wait_ge(gained_done, len(OUT_PARTS[0]) * (t + 1))
                act.wait_ge(out_rstd_done, t + 1)
                act.activation(res[:, t, 0:columns], gained[:, t, 0:columns], ACT.Copy,
                               scale=out_rstd[:, t:t + 1]).then_inc(scaled_act_done, 1)

            squares_of_part(0, 0)
            squares_of_part(0, 1)
            scale_tile(0, D)
            squares_of_part(1, 0)
            squares_of_part(1, 1)
            scale_tile(1, SCALED_BY_ACT)
            act.wait_ge(scaled_act_done, TT)
            act.dma_start(out[P:, 0:SCALED_BY_ACT], res[:, 1, 0:SCALED_BY_ACT]).then_inc(stored, 16)

        @block.vector
        def _(dve):
            def split_lo(c, slice_=None):
                dve.wait_ge(w_hi_done, splits(c) if slice_ is None else splits(c, slice_))
                if c >= SPLIT:
                    dve.wait_ge(chunk_used, c - SPLIT + 1)
                part = slice(None) if slice_ is None else slice(slice_ * WIDTH, (slice_ + 1) * WIDTH)
                dve.tensor_tensor(w_lo[:, c % SPLIT, part], w_raw[:, c % RAW, part],
                                  w_hi[:, c % SPLIT, part].bitcast(fp32),
                                  ALU.subtract).then_inc(w_lo_done, 1)

            def split_x_lo(k):
                dve.wait_ge(x_hi_done, k + 1)
                dve.scalar_tensor_tensor(x_lo[:, k, :], xt[:, k, :], gain_col[:, k:k + 1],
                                         x_hi[:, k, :].bitcast(fp32), ALU.mult,
                                         ALU.subtract).then_inc(x_lo_done, 1)

            def make_diag():
                dve.wait_ge(rstd_done, 1)
                dve.wait_ge(consts_done, 2)
                for t in range(TT):
                    dve.tensor_scalar(rstd_diag[:, t * P:(t + 1) * P], ident[:, :], rstd[:, t:t + 1],
                                      None, ALU.mult).then_inc(diag_done, 1)

            def make_tables():
                dve.wait_ge(bcast_done, 1)
                dve.tensor_copy(rstd_row[:, :], bank[PV_BANK][:, 0:SEQ]).then_inc(rstd_row_done, 1)
                dve.wait_ge(rstd_row_done, 1)
                dve.wait_ge(table_loaded, 16)
                dve.tensor_tensor(rope_scaled[:, :, :], table[:, :, :], over(rstd_row, 2),
                                  ALU.mult).then_inc(tables_done, 1)

            def over(row, n):
                return row[:, :].unsqueeze(1).broadcast_to([P, n, SEQ])

            def rotate(n):
                read = 2 * (n % 2) + n // 2
                src = unrotated[:, read, :, :]
                dve.wait_ge(qk_read, read + 1)
                dve.wait_ge(tables_done, 1)
                if n > 0:
                    dve.wait_ge(roped_done, n)
                dve.tensor_tensor(rope_sin[:, :, :], src, rope_scaled[:, 1:2, :].broadcast_to([P, 2, SEQ]),
                                  ALU.mult).then_inc(products_done, 1)
                dve.wait_ge(products_done, 2 * n + 1)
                dve.tensor_tensor(src, src, rope_scaled[:, 0:1, :].broadcast_to([P, 2, SEQ]),
                                  ALU.mult).then_inc(products_done, 1)
                dve.wait_ge(products_done, 2 * (n + 1))
                dve.tensor_tensor(roped[:, n, 0, :], src[:, 0, :], rope_sin[:, 1, :], ALU.subtract)
                dve.tensor_tensor(roped[:, n, 1, :], src[:, 1, :], rope_sin[:, 0, :],
                                  ALU.add).then_inc(roped_done, 1)

            def mask_and_max(h):
                dve.wait_ge(scores_done, h + 1)
                if h >= PROBS:
                    dve.wait_ge(pt_done, h - PROBS + 1)
                b = bank[SCORES_BANK[h % 2]]
                for t in range(TT):
                    cols, m = (slice(0, P), slice(P, 2 * P)) if t == 0 else (slice(P, BLK), slice(0, 2 * P))
                    dve.tensor_tensor_reduce(out=probs[:, h % PROBS, cols], in0=b[:, cols], in1=mask[:, m],
                                             scale=-SCALE, scalar=-MASKED, op0=ALU.add, op1=ALU.min,
                                             accum_out=neg_max[:, h, t:t + 1]).then_inc(masked_done, 1)

            def normalise(h):
                dve.wait_ge(exp_done, TT * (h + 1))
                dve.reciprocal(denom_recip[:, h, :], denom[:, h, :]).then_inc(recip_done, 1)
                dve.wait_ge(recip_done, h + 1)
                for t in range(TT):
                    cols = slice(0, P) if t == 0 else slice(P, BLK)
                    dve.tensor_scalar(probs[:, h % PROBS, cols], probs[:, h % PROBS, cols],
                                      denom_recip[:, h, t:t + 1], None, ALU.mult).then_inc(norm_done, 1)

            def read_rows(place, dst, done):
                dve.wait_ge(chunk_used, chunks_to(place))
                for i, b in enumerate(BLOCK_BANKS[place % 2]):
                    dve.tensor_tensor(dst[:, 2 * i:2 * i + 2, :],
                                      bank[b][:, :].rearrange("p (f n) -> p f n", f=2), over(rstd_row, 2),
                                      ALU.mult).then_inc(done, 1)

            sums = (sum_a, sum_b)

            def double(g):
                src, dst, shift = (u_pad if g == 0 else sums[(g - 1) % 2]), sums[g % 2], 1 << g
                lo = 2 * shift - 1
                dve.wait_ge(u_done, 2)
                if g > 0:
                    dve.wait_ge(sums_done, g)
                dve.tensor_tensor(dst[:, g:GROUPS, lo:], src[:, g:GROUPS, lo:],
                                  src[:, g:GROUPS, lo - shift:PAD + SEQ - shift],
                                  ALU.add).then_inc(sums_done, 1)

            def pool_minus_token(g):
                dve.wait_ge(sums_done, GROUPS)
                dve.wait_ge(pool_consts_loaded, 16 * 4)
                s = sums[g % 2]
                dve.tensor_tensor(edge_mean[:, g, :], s[:, g, PAD:PAD + EDGE], edge_recip[:, g, :],
                                  ALU.mult).then_inc(edge_done, 1)
                dve.scalar_tensor_tensor(pooled[:, g, EDGE:], s[:, g, PAD + EDGE:], 1.0 / WINDOWS[g],
                                         u_pad[:, g, PAD + EDGE:], ALU.mult,
                                         ALU.subtract).then_inc(pooled_done, 1)
                dve.wait_ge(edge_done, g + 1)
                dve.tensor_tensor(pooled[:, g, 0:EDGE], edge_mean[:, g, :], u_pad[:, g, PAD:PAD + EDGE],
                                  ALU.subtract).then_inc(pooled_done, 1)


            def bias_and_gate(g):
                dve.wait_ge(wpool_done, g // 2 + 1)
                dve.wait_ge(gate_done, 2)
                dve.scalar_tensor_tensor(pooled[:, g, :], bank[POOL_BANKS[g // 2]][:, (g % 2) * SEQ:(g % 2 + 1) * SEQ],
                                         b_col[:, g:g + 1], gate[:, g, :], ALU.add,
                                         ALU.mult).then_inc(pool_gated, 1)

            def gate_attention():
                dve.wait_ge(pv_read, GROUPS)
                dve.wait_ge(gate_done, 4)
                dve.tensor_tensor(attn[:, :, :], attn[:, :, :], gate[:, :, :], ALU.mult).then_inc(attn_gated, 1)

            def mix(k):
                g = k % GROUPS
                if k < GROUPS:
                    dve.wait_ge(sigm_done, 1)
                    dve.wait_ge(pool_gated, g + 1)
                    dve.scalar_tensor_tensor(mixed[:, k, :], pooled[:, g, :], scale_col[:, g:g + 1], sigm[:, g, :],
                                             ALU.mult, ALU.mult).then_inc(mixed_done, 1)
                else:
                    dve.wait_ge(sigm_done, 2)
                    dve.wait_ge(attn_gated, 1)
                    dve.tensor_tensor(mixed[:, k, :], attn[:, g, :], sigm[:, g, :],
                                      ALU.mult).then_inc(mixed_done, 1)

            def split_mixed_lo(k):
                dve.wait_ge(mixed_hi_done, k + 1)
                dve.tensor_tensor(mixed_lo[:, k, :], mixed[:, k, :], mixed_hi[:, k, :].bitcast(fp32),
                                  ALU.subtract).then_inc(mixed_lo_done, 1)

            dve.wait_ge(gain_loaded, 16)
            split_x_lo(0)
            split_lo(0, 0)
            split_x_lo(1)
            split_lo(0, 1)
            split_x_lo(2)
            split_lo(1, 0)
            split_x_lo(3)
            split_lo(1, 1)
            split_x_lo(4)
            split_x_lo(5)
            split_lo(2)
            split_x_lo(6)
            split_x_lo(7)
            split_lo(3)
            for s in range(STEPS):
                if s == 4:
                    make_diag()
                if s == 8:
                    make_tables()
                if s in ROTATE_AT:
                    rotate(ROTATE_AT.index(s))
                if (h := head_at(softmax_at, s)) is not None:
                    mask_and_max(h)
                if (h := head_at(normalise_at, s)) is not None:
                    normalise(h)
                if s == 32:
                    read_rows(U, u_pad[:, :, PAD:], u_done)
                if s in (33, 34, 35, 36):
                    double(s - 33)
                if s in (37, 38, 39, 40):
                    pool_minus_token(s - 37)
                if s == 40:
                    read_rows(GP, gate, gate_done)
                if s == 44:
                    for g in range(GROUPS):
                        bias_and_gate(g)
                if s == 48:
                    dve.wait_ge(pool_gated, GROUPS)
                    dve.wait_ge(sigm_done, 1)
                    read_rows(GA, gate, gate_done)
                if s == 49:
                    gate_attention()
                if s % 2 == 0 and (c := (s + AHEAD) // 2) < CHUNKS:
                    split_lo(c)
                if s in (45, 51):
                    first = 0 if s == 45 else GROUPS
                    for k in range(first, first + GROUPS):
                        mix(k)
                        if k > first:
                            split_mixed_lo(k - 1)
                    split_mixed_lo(first + GROUPS - 1)

            def add_residual(t, i):
                at, size, b = OUT_PARTS[t][i]
                dve.wait_ge(out_done, len(OUT_PARTS[0]) * t + i + 1)
                dve.tensor_tensor(res[:, t, at:at + size], bank[b][:, 0:size],
                                  res[:, t, at:at + size], ALU.add).then_inc(added_done, 1)

            def apply_gain(t, i):
                at, size, _ = OUT_PARTS[t][i]
                dve.wait_ge(added_done, len(OUT_PARTS[0]) * t + i + 1)
                dve.tensor_tensor(gained[:, t, at:at + size], res[:, t, at:at + size], final_row[:, at:at + size],
                                  ALU.mult).then_inc(gained_done, 1)

            def add_means(t, target):
                dve.wait_ge(out_square_done, 2 * (t + 1))
                return dve.tensor_scalar(target, out_square[:, t, 0:1], out_square[:, t, 1:2], EPS, ALU.add, ALU.add)

            dve.wait_ge(final_loaded, 16)
            for i in range(2):
                add_residual(0, i)
                apply_gain(0, i)
            add_means(0, out_mean[:, 0:1]).then_inc(out_mean_done, 1)
            for i in range(2):
                add_residual(1, i)
                apply_gain(1, i)
            add_means(1, mean_others[:, :]).then_inc(mean_others_done, 1)
            add_residual(1, 2)
            dve.wait_ge(added_done, 5)
            dve.wait_ge(mean_others_done, 1)
            at = OUT_PARTS[1][2][0]
            dve.tensor_tensor_reduce(out=last_square, in0=res[:, 1, at:], in1=res[:, 1, at:],
                                     scale=1.0 / D, scalar=mean_others[:, 0:1], op0=ALU.mult, op1=ALU.add,
                                     accum_out=out_mean[:, 1:2]).then_inc(out_mean_done, 1)
            apply_gain(1, 2)
            dve.wait_ge(gained_done, 5)
            dve.wait_ge(out_rstd_done, 2)
            dve.tensor_scalar(res[:, 1, SCALED_BY_ACT:], gained[:, 1, SCALED_BY_ACT:], out_rstd[:, 1:2], None,
                              ALU.mult).then_inc(scaled_done, 1)

        @block.tensor
        def _(pe):
            PASSES = ((w_hi, 0), (w_hi, 1), (w_lo, 0))

            def wait_for_split(c, slice_, lo):
                if c < FINE or slice_ == 0:
                    pe.wait_ge(w_lo_done if lo else w_hi_done, splits(c, slice_))

            def wait_for_banks(place):
                if place == V:
                    pe.wait_ge(qk_read, 2)
                if place == U:
                    pe.wait_ge(qk_read, 4)
                if place == GP:
                    pe.wait_ge(v_done, TT)
                if place == GA:
                    pe.wait_ge(u_done, 2)

            def project(s):
                place, k, c = s // KT, s % KT, s // 2
                if k == 0:
                    wait_for_banks(place)
                for n, (w, lo) in enumerate(PASSES):
                    if n != 1:
                        wait_for_split(c, s % 2, lo=(n == 2))
                    if place == Q and n < 2:
                        pe.wait_ge((x_hi_done, x_lo_done)[n], k + 1)
                    act, tile = (x_hi, x_lo)[lo], halves(w[:, c % SPLIT, :])[:, k % 2, :]
                    first, last = k == 0 and n == 0, k == KT - 1 and n == 2
                    if place == V:
                        for t in range(TT):
                            mm = pe.matmul(bank[BLOCK_BANKS[0][t]][:, :], act[:, k, t * P:(t + 1) * P], tile,
                                           start=first, stop=last, skip_group_check=True)
                        continue
                    for i in range(4):
                        cols = tile[:, i * P:(i + 1) * P]
                        mm = pe.matmul(bank[BLOCK_BANKS[place % 2][i // 2]][:, (i % 2) * SEQ:(i % 2 + 1) * SEQ],
                                       cols, act[:, k, :], start=first and i % 2 == 0, stop=last,
                                       skip_group_check=True)
                return mm

            def project_out(k, t, n, parts):
                c, (w, lo) = IN_CHUNKS + k, PASSES[n]
                pe.wait_ge(w_lo_done if n == 2 else w_hi_done, splits(c))
                if n < 2:
                    pe.wait_ge((mixed_hi_done, mixed_lo_done)[n], k + 1)
                for at, size, b in parts:
                    mm = pe.matmul(bank[b][:, 0:size], (mixed_hi, mixed_lo)[lo][:, k, t * P:(t + 1) * P],
                                   w[:, c % SPLIT, at:at + size], start=(k == 0 and n == 0),
                                   stop=(k == KT - 1 and n == 2), skip_group_check=True)
                return mm

            def scores(h):
                n, at = h // 4, HEAD_DIM * (h % 2)
                pe.wait_ge(qk_moved[2 * n], 16 * 4)
                pe.wait_ge(qk_moved[2 * n + 1], 16 * 4)
                if h >= 2:
                    pe.wait_ge(masked_done, TT * (h - 1))
                b = bank[SCORES_BANK[h % 2]]
                q_h, k_h = (qk[at:at + HEAD_DIM, i, h // 2, :] for i in range(2))
                pe.matmul(b[:, 0:P], q_h[:, 0:P], k_h[:, 0:P], start=True, stop=True)
                pe.matmul(b[:, P:BLK], q_h[:, P:SEQ], k_h, start=True,
                          stop=True).then_inc(scores_done, 1)

            def transpose(h):
                pe.wait_ge(norm_done, TT * (h + 1))
                if h > 0:
                    pe.wait_ge(pt_read, h)
                for i in range(3):
                    mm = pe.transpose(bank[PT_BANK][:, i * P:(i + 1) * P],
                                      probs[:, h % PROBS, i * P:(i + 1) * P], ident[:, :])
                mm.then_inc(pt_done, 1)

            def attend(h):
                at = HEAD_DIM * (h % 2)
                pe.wait_ge(v_done, TT)
                pe.wait_ge(pt_read, h + 1)
                if h >= 2:
                    pe.wait_ge(pv_read, h // 2)
                o, pt = bank[PV_BANK][at:at + HEAD_DIM, :], probs_t[:, h % PROBS_T, :]
                v_h = v[:, :, h * HEAD_DIM:(h + 1) * HEAD_DIM]
                pe.matmul(o[:, 0:SEQ], v_h[:, 0, :], pt[:, 0:SEQ], start=True, stop=False)
                pe.matmul(o[:, P:SEQ], v_h[:, 1, :], pt[:, SEQ:BLK], start=False,
                          stop=True).then_inc(pv_done, 1)

            def broadcast_rstd():
                for t in range(TT):
                    pe.wait_ge(diag_done, t + 1)
                    mm = pe.matmul(bank[PV_BANK][:, t * P:(t + 1) * P], ones[:, :],
                                   rstd_diag[:, t * P:(t + 1) * P], start=True, stop=True)
                mm.then_inc(bcast_done, 1)

            def pool_weights(i):
                pe.wait_ge(gate_done, i + 1)
                pe.wait_ge(pool_consts_loaded, 16 * 4)
                for g in (2 * i, 2 * i + 1):
                    pe.wait_ge(pooled_done, 2 * (g + 1))
                    mm = pe.matmul(bank[POOL_BANKS[i]][:, (g % 2) * SEQ:(g % 2 + 1) * SEQ], wp[:, g, :],
                                   pooled[:, g, :], start=True, stop=True)
                mm.then_inc(wpool_done, 1)

            pe.wait_ge(memset_done, 1)
            for _ in range(WARM_UP):
                pe.matmul(bank[PT_BANK][:, 0:P], ones[:, :], ones[:, :], start=True, stop=True)
            for s in range(OUT_STEP):
                mm = project(s)
                if s % 2 == 1:
                    mm.then_inc(chunk_used, 1)
                if s == 11:
                    broadcast_rstd()
                if (h := head_at(scores_at, s)) is not None:
                    scores(h)
                if (h := head_at(transpose_at, s)) is not None:
                    transpose(h)
                if (h := head_at(attend_at, s)) is not None:
                    attend(h)
                if s in (42, 43):
                    pool_weights(s - 42)
            pe.wait_ge(pool_gated, GROUPS)
            pe.wait_ge(pv_read, HEADS // 2)
            for k in range(KT - TAIL):
                for t in range(TT):
                    for n in range(len(PASSES)):
                        mm = project_out(k, t, n, OUT_PARTS[t])
                mm.then_inc(chunk_used, 1)
            for t in range(TT):
                for part in OUT_PARTS[t]:
                    for k in range(KT - TAIL, KT):
                        for n in range(len(PASSES)):
                            mm = project_out(k, t, n, (part,))
                    mm.then_inc(out_done, 1)


def kernel(**inputs):
    import concourse.bacc as bacc
    from concourse.bass_utils import run_bass_kernel_spmd

    inputs = {name: np.asarray(a) for name, a in inputs.items()}
    x = np.ascontiguousarray(inputs["x"])[0]
    arrays = {
        "x": x,
        "x_t": np.ascontiguousarray(x.T),
        "gain": np.ascontiguousarray(inputs["norm_gain"][0].reshape(KT, P).T),
        "w_in": rotary_columns_together(inputs["w_in"][0]),
        "w_pool": np.ascontiguousarray(inputs["w_pool"][0]),
        "b_pool": np.ascontiguousarray(inputs["b_pool"][0].T),
        "pool_scale": np.ascontiguousarray(inputs["pool_scale"][0].reshape(GROUPS, P).T),
        "w_out": np.ascontiguousarray(inputs["w_out"][0]),
        "final_gain": np.ascontiguousarray(inputs["final_gain"]),
        "rope_table": rope_constants(),
        "edge_table": edge_constants(),
    }
    nc = bacc.Bacc("TRN2", target_bir_lowering=False, num_devices=1)
    args = [nc.dram_tensor("in_" + name, a.shape, mybir.dt.from_np(a.dtype), kind="ExternalInput").ap()
            for name, a in arrays.items()]
    out = nc.dram_tensor("out_dram", (SEQ, D), mybir.dt.float32, kind="ExternalOutput").ap()
    hymba_kernel(nc, *args, out)
    r = run_bass_kernel_spmd(nc, [{"in_" + name: a for name, a in arrays.items()}], core_ids=[0])
    return r.results[0]["out_dram"].reshape(1, SEQ, D)


def rotary_columns_together(w_in):
    qk = w_in[:, :2 * WIDTH].reshape(D, 2, 2, 4, 2, HALF).transpose(0, 1, 2, 4, 3, 5)
    return np.ascontiguousarray(np.concatenate([qk.reshape(D, 2 * WIDTH), w_in[:, 2 * WIDTH:]], axis=1))


def rope_constants():
    inv_freq = (np.float32(1.0) / np.float32(THETA) ** (np.arange(0, HEAD_DIM, 2, dtype=np.float32)
                                                        / np.float32(HEAD_DIM))).astype(np.float32)
    angle = inv_freq[:, None] * np.arange(SEQ, dtype=np.float32)[None, :]
    both = np.stack([np.cos(angle), np.sin(angle)], axis=1).astype(np.float32)
    return np.ascontiguousarray(np.tile(both, (P // HALF, 1, 1)))


def edge_constants():
    counts = np.minimum(np.arange(1, EDGE + 1)[None, :], np.array(WINDOWS)[:, None])
    one = (np.float32(1.0) / counts.astype(np.float32)).astype(np.float32)
    return np.ascontiguousarray(np.broadcast_to(one, (P, GROUPS, EDGE)))
```

```python
import concourse.bass as bass
from concourse import mybir
from contextlib import ExitStack

import numpy as np

SEQ, D = 256, 1024
HEADS, HEAD_DIM = 8, 64
WIDTH = HEADS * HEAD_DIM
BLOCKS = 6
WINDOWS = (2, 4, 8, 16)
GROUPS = len(WINDOWS)
EPS = 1e-6
THETA = 10000.0
P = 128
KT = D // P
TT = SEQ // P
HALF = HEAD_DIM // 2
WARM_UP = 8
EDGE = max(WINDOWS)


def hymba_kernel(nc, x, x_t, gain, w_in, w_pool, b_pool, pool_scale, w_out, final_gain,
                 rope_table, edge_table, out):
    fp32, fp32r = mybir.dt.float32, mybir.dt.float32r
    ALU, ACT = mybir.AluOpType, mybir.ActivationFunctionType

    ORDER = [0, 1, 2, 4, 5, 3]
    Q, K, V, U, GP, GA = range(BLOCKS)
    CHUNK = 1024
    PER_BLOCK = KT * WIDTH // CHUNK
    IN_CHUNKS = BLOCKS * PER_BLOCK
    CHUNKS = IN_CHUNKS + KT
    RAW, SPLIT = 8, 5
    FINE = PER_BLOCK
    PIECES = [(0, 0, WIDTH // 2), (0, WIDTH // 2, WIDTH // 2)] + [
        (i // 2, i % 2 * WIDTH, WIDTH) for i in range(1, 2 * FINE)]
    STEPS = 2 * CHUNKS
    OUT_STEP = 2 * IN_CHUNKS
    AHEAD = 8

    FIRST = 27
    SPLIT_HEADS_AT = (22, 32)
    def scores_at(pair): return FIRST + 4 * pair
    def softmax_at(h): return FIRST + 2 * h + 1
    def exp_at(h): return FIRST + 2 * h + 2
    def normalise_at(h): return FIRST + 2 * h + 3
    def transpose_at(h): return FIRST + 2 * h + 4
    def evacuate_at(h): return FIRST + 2 * h + 5
    def attend_at(pair): return FIRST + 4 * pair + 8
    def read_attn_at(pair): return attend_at(pair) + 1

    SQUARES_AT, DIAG_AT, BROADCAST_AT, TABLES_AT = 2, 4, 11, 8
    READ_QK_AT = (8, 9, 16, 17)
    ROTATE_AT = (9, 16, 18, 20)
    READ_V_AT, READ_U_AT = 24, 32
    DOUBLE_AT = (34, 35, 36, 37)
    POOL_AT = (38, 39, 40, 41)
    POOL_WEIGHTS_AT = (42, 43)
    READ_GATE_AT = (40, 48)
    GATE_BRANCH_AT = (44, 49)
    SIGMOID_AT = (43, 51)
    MIX_AT = (45, 51)
    SPLIT_MIXED_HI_AT = (46, 52)

    def head_at(step_of, s, count=HEADS):
        return next((h for h in range(count) if step_of(h) == s), None)

    def pair_at(step_of, s):
        return head_at(step_of, s, HEADS // 2)

    SCALE = HEAD_DIM ** -0.5
    MASKED = -3.0e38

    ctx = ExitStack()
    with ctx:
        def sb(name, shape, dt=fp32):
            return ctx.enter_context(nc.sbuf_tensor(name, shape, dt))

        def sem(name):
            return ctx.enter_context(nc.semaphore(name))

        w_raw = sb("w_raw", [P, RAW, CHUNK])
        w_hi = sb("w_hi", [P, SPLIT, CHUNK], fp32r)
        w_lo = sb("w_lo", [P, SPLIT, CHUNK], fp32r)
        xt = sb("xt", [P, KT, SEQ])
        x_hi = sb("x_hi", [P, KT, SEQ], fp32r)
        x_lo = sb("x_lo", [P, KT, SEQ], fp32r)
        gain_col = sb("gain_col", [P, KT])
        res = sb("res", [P, TT, D])
        table = sb("table", [P, 2, SEQ])
        edge_recip = sb("edge_recip", [P, GROUPS, EDGE])
        ident = sb("ident", [P, P])
        ones = sb("ones", [P, P])
        mask = sb("mask", [P, 2 * P])
        neg_half = sb("neg_half", [P, TT])
        warm = sb("warm", [P, TT])
        wp = sb("wp", [P, GROUPS, P])
        b_col = sb("b_col", [P, GROUPS])
        scale_col = sb("scale_col", [P, GROUPS])
        final_row = sb("final_row", [P, D])
        square_sum = sb("square_sum", [P, TT])
        mean_square = sb("mean_square", [P, TT])
        rstd = sb("rstd", [P, TT])
        rstd_diag = sb("rstd_diag", [P, SEQ])
        rstd_row = sb("rstd_row", [P, SEQ])
        rope_scaled = sb("rope_scaled", [P, 2, SEQ])
        unrotated = sb("unrotated", [P, 4, 2, SEQ])
        roped = sb("roped", [P, 4, 2, SEQ])
        qk = sb("qk", [P, 2, HEADS // 2, SEQ])
        v = sb("v", [P, TT, WIDTH])
        BLK = 3 * P
        PROBS, PROBS_T = 3, 2
        probs = sb("probs", [P, PROBS, BLK])
        neg_max = sb("neg_max", [P, HEADS, TT])
        denom = sb("denom", [P, HEADS, TT])
        denom_recip = sb("denom_recip", [P, HEADS, TT])
        probs_t = sb("probs_t", [P, PROBS_T, BLK])
        attn = sb("attn", [P, GROUPS, SEQ])
        rope_sin = attn[:, 0:2, :]
        gate = sb("gate", [P, GROUPS, SEQ])
        sigm = sb("sigm", [P, GROUPS, SEQ])
        PAD = EDGE
        u_pad = sb("u_pad", [P, GROUPS, PAD + SEQ])
        sum_a = sb("sum_a", [P, GROUPS, PAD + SEQ])
        sum_b = sb("sum_b", [P, GROUPS, PAD + SEQ])
        edge_mean = sb("edge_mean", [P, GROUPS, EDGE])
        pooled = sb("pooled", [P, GROUPS, SEQ])
        mixed = sb("mixed", [P, KT, SEQ])
        mixed_hi = sb("mixed_hi", [P, KT, SEQ], fp32r)
        mixed_lo = sb("mixed_lo", [P, KT, SEQ], fp32r)
        q_hi, q_lo = (tile[:, 4:6, :].rearrange("p a (b n) -> p (a b) n", b=2) for tile in (mixed_hi, mixed_lo))
        k_hi, k_lo = mixed_hi[:, 0:4, :], mixed_lo[:, 0:4, :]
        out_square = sb("out_square", [P, TT, 2])
        out_mean = sb("out_mean", [P, TT])
        mean_others = sb("mean_others", [P, 1])
        square_out = [tile[:, :, :].rearrange("p g n -> p (g n)") for tile in (attn, sigm)]
        last_square = gate[:, 0, :]
        gained = mixed[:, :, :].rearrange("p (t k) n -> p t (k n)", t=TT)
        out_rstd = sb("out_rstd", [P, TT])

        bank = [ctx.enter_context(nc.psum_tensor(f"bank{i}", [P, 512], fp32)) for i in range(8)]
        BLOCK_BANKS = [(0, 1), (2, 3)]
        SCORES_BANK, PT_BANK, PV_BANK = (4, 5), 6, 7
        POOL_BANKS = (0, 1)
        OUT_PARTS = (((0, 512, 0), (512, 512, 1)), ((0, 512, 4), (512, 256, 5), (768, 256, 7)))
        TAIL = 4
        SCALED_BY_ACT, SCALED_BY_DVE = 320, ((320, 640), (640, D))

        raw_loaded = [sem(f"raw_loaded{i}") for i in range(RAW)]
        piece_loaded = [sem(f"piece_loaded{i}") for i in range(len(PIECES))]
        XT_PARTS = ((0, 1), (1, 2), (2, 4), (4, 6), (6, KT))
        xt_loaded = [sem(f"xt_loaded{i}") for i in range(len(XT_PARTS))]
        gain_loaded = sem("gain_loaded")
        table_loaded = sem("table_loaded")
        res_loaded = [sem(f"res_loaded{i}") for i in range(TT)]
        pool_consts_loaded = sem("pool_consts_loaded")
        final_loaded = sem("final_loaded")
        qk_moved = [sem(f"qk_moved{i}") for i in range(4)]
        x_hi_done, x_lo_done = sem("x_hi_done"), sem("x_lo_done")
        w_hi_done, w_lo_done = sem("w_hi_done"), sem("w_lo_done")
        chunk_used = sem("chunk_used")
        ones_done, memset_done, consts_done = sem("ones_done"), sem("memset_done"), sem("consts_done")
        square_done, mean_done, rstd_done = sem("square_done"), sem("mean_done"), sem("rstd_done")
        diag_done, bcast_done, rstd_row_done = sem("diag_done"), sem("bcast_done"), sem("rstd_row_done")
        tables_done = sem("tables_done")
        qk_read, products_done, roped_done = sem("qk_read"), sem("products_done"), sem("roped_done")
        v_done = sem("v_done")
        heads_hi_done, heads_lo_done = sem("heads_hi_done"), sem("heads_lo_done")
        scores_done, masked_done, exp_done = sem("scores_done"), sem("masked_done"), sem("exp_done")
        recip_done, norm_done = sem("recip_done"), sem("norm_done")
        pt_done, pt_read, pv_done, pv_read = sem("pt_done"), sem("pt_read"), sem("pv_done"), sem("pv_read")
        u_done, sums_done = sem("u_done"), sem("sums_done")
        edge_done, pooled_done = sem("edge_done"), sem("pooled_done")
        wpool_done, pool_gated = sem("wpool_done"), sem("pool_gated")
        gate_done, sigm_done, attn_gated = sem("gate_done"), sem("sigm_done"), sem("attn_gated")
        mixed_done, mixed_hi_done, mixed_lo_done = sem("mixed_done"), sem("mixed_hi_done"), sem("mixed_lo_done")
        out_done, added_done, out_square_done = sem("out_done"), sem("added_done"), sem("out_square_done")
        out_mean_done, out_rstd_done = sem("out_mean_done"), sem("out_rstd_done")
        gained_done, scaled_done = sem("gained_done"), sem("scaled_done")
        scaled_act_done, mean_others_done = sem("scaled_act_done"), sem("mean_others_done")
        stored = sem("stored")

        def splits(c):
            return 2 * c + 3 if c < FINE else c + 2 + FINE

        def splits_to(c, column):
            return next(i + 1 for i, (pc, at, size) in enumerate(PIECES) if pc == c and column < at + size)

        def chunks_to(place):
            return PER_BLOCK * (place + 1)

        block = ctx.enter_context(nc.Block())

        @block.sync
        def _(sp):
            def load_chunk(c):
                slot = w_raw[:, c % RAW, :]
                if c >= RAW:
                    sp.wait_ge(w_lo_done, splits(c - RAW))
                if c < IN_CHUNKS:
                    b, j = ORDER[c // PER_BLOCK], c % PER_BLOCK
                    rows = w_in[2 * j * P:2 * (j + 1) * P, b * WIDTH:(b + 1) * WIDTH]
                    src, dst = rows.rearrange("(s p) n -> p s n", p=P), slot.rearrange("p (s n) -> p s n", s=2)
                else:
                    rows = (c - IN_CHUNKS + GROUPS) % KT
                    src, dst = w_out[rows * P:(rows + 1) * P, :], slot
                sp.dma_start(dst, src).then_inc(raw_loaded[c % RAW], 16)

            def load_piece(i):
                c, at, size = PIECES[i]
                k, col = 2 * c + at // WIDTH, at % WIDTH
                sp.dma_start(w_raw[:, c, at:at + size], w_in[k * P:(k + 1) * P, col:col + size]).then_inc(
                    piece_loaded[i], 16)

            def load_res(t):
                sp.dma_start(res[:, t, :], x[t * P:(t + 1) * P, :]).then_inc(res_loaded[t], 16)

            def load_xt(i):
                lo, hi = XT_PARTS[i]
                sp.dma_start(xt[:, lo:hi, :], x_t.rearrange("(k p) n -> p k n", p=P)[:, lo:hi, :]).then_inc(
                    xt_loaded[i], 16)

            load_xt(0)
            load_piece(0)
            load_piece(1)
            load_xt(1)
            load_piece(2)
            load_xt(2)
            load_piece(3)
            load_piece(4)
            load_xt(3)
            load_piece(5)
            load_piece(6)
            load_xt(4)
            load_piece(7)
            load_piece(8)
            load_chunk(4)
            load_res(0)
            load_chunk(5)
            load_res(1)
            load_chunk(6)
            sp.dma_start(table[:, :, :], rope_table).then_inc(table_loaded, 16)

            def move_heads(n):
                sp.wait_ge(roped_done, n + 1)
                for pair in range(2):
                    for f in range(2):
                        sp.dma_start(qk[f:P:2, n % 2, 2 * (n // 2) + pair, :],
                                     roped[HEAD_DIM * pair:HEAD_DIM * (pair + 1), n, f, :]).then_inc(qk_moved[n], 16)

            for c in range(7, CHUNKS):
                if c == 17:
                    move_heads(0)
                    move_heads(1)
                if c in (19, 20):
                    move_heads(c - 17)
                load_chunk(c)
                if c == 21:
                    sp.dma_start(wp[:, :, :], w_pool.rearrange("g c d -> c g d")).then_inc(pool_consts_loaded, 16)
                    sp.dma_start(b_col[:, :], b_pool).then_inc(pool_consts_loaded, 16)
                    sp.dma_start(scale_col[:, :], pool_scale).then_inc(pool_consts_loaded, 16)
                    sp.dma_start(edge_recip[:, :, :], edge_table).then_inc(pool_consts_loaded, 16)
                    sp.dma_start(final_row[:, :], final_gain.partition_broadcast(P)).then_inc(final_loaded, 16)
            sp.wait_ge(scaled_act_done, 1)
            sp.dma_start(out[0:P, :], res[:, 0, :]).then_inc(stored, 16)
            for i, (lo, hi) in enumerate(SCALED_BY_DVE):
                sp.wait_ge(scaled_done, i + 1)
                sp.dma_start(out[P:, lo:hi], res[:, 1, lo:hi]).then_inc(stored, 16)
            sp.wait_ge(stored, 16 * (2 + len(SCALED_BY_DVE)))

        @block.gpsimd
        def _(pool):
            pool.memset(ident[:, :], 0.0).then_inc(memset_done, 1)
            pool.memset(mask[:, :], 0.0).then_inc(memset_done, 1)
            pool.memset(neg_half[:, :], -0.5).then_inc(memset_done, 1)
            pool.memset(u_pad[:, :, 0:PAD], 0.0).then_inc(memset_done, 1)
            pool.wait_ge(memset_done, 4)
            pool.affine_select(out=ident[:, :], in_=ident[:, :], compare_op=ALU.not_equal, fill=1.0,
                               base=0, pattern=[[-1, P]], channel_multiplier=1).then_inc(consts_done, 1)
            pool.affine_select(out=mask[:, P:2 * P], in_=mask[:, P:2 * P], compare_op=ALU.is_ge,
                               fill=MASKED, base=0, pattern=[[-1, P]],
                               channel_multiplier=1).then_inc(consts_done, 1)

            pool.wait_ge(square_done, TT)
            pool.tensor_scalar(mean_square[:, :], square_sum[:, :], EPS, None,
                               ALU.add).then_inc(mean_done, 1)
            pool.wait_ge(mean_done, 1)
            pool.tensor_tensor(rstd[:, :], mean_square[:, :], neg_half[:, :],
                               ALU.pow).then_inc(rstd_done, 1)

            for t in range(TT):
                pool.wait_ge(out_mean_done, t + 1)
                pool.tensor_tensor(out_rstd[:, t:t + 1], out_mean[:, t:t + 1], neg_half[:, 0:1],
                                   ALU.pow).then_inc(out_rstd_done, 1)

        @block.scalar
        def _(act):
            def split_hi(c):
                loads = c // RAW + (c % RAW >= FINE)
                act.wait_ge(raw_loaded[c % RAW], 16 * loads)
                if c >= SPLIT:
                    act.wait_ge(chunk_used, c - SPLIT + 1)
                act.activation(w_hi[:, c % SPLIT, :], w_raw[:, c % RAW, :], ACT.Copy).then_inc(w_hi_done, 1)

            def split_piece_hi(i):
                c, at, size = PIECES[i]
                act.wait_ge(piece_loaded[i], 16)
                act.activation(w_hi[:, c, at:at + size], w_raw[:, c, at:at + size], ACT.Copy).then_inc(w_hi_done, 1)

            def split_x_hi(k):
                act.wait_ge(xt_loaded[next(i for i, (lo, hi) in enumerate(XT_PARTS) if lo <= k < hi)], 16)
                act.activation(x_hi[:, k, :], xt[:, k, :], ACT.Copy,
                               scale=gain_col[:, k:k + 1]).then_inc(x_hi_done, 1)

            def squares(t):
                act.wait_ge(res_loaded[t], 16)
                act.activation(mixed[:, 4 * t:4 * t + 4, :], res[:, t, :].rearrange("p (k n) -> p k n", k=4),
                               ACT.Square, scale=D ** -0.5, accum_out=square_sum[:, t:t + 1]).then_inc(square_done, 1)

            def split_heads_hi(n):
                pairs = slice(2 * n, 2 * n + 2)
                act.wait_ge(qk_moved[2 * n], 16 * 4)
                act.wait_ge(qk_moved[2 * n + 1], 16 * 4)
                act.activation(q_hi[:, pairs, :], qk[:, 0, pairs, P:SEQ], ACT.Copy).then_inc(heads_hi_done, 1)
                act.activation(k_hi[:, pairs, :], qk[:, 1, pairs, :], ACT.Copy).then_inc(heads_hi_done, 1)

            def exps(h):
                act.wait_ge(masked_done, TT * (h + 1))
                for t in range(TT):
                    cols = slice(0, P) if t == 0 else slice(P, BLK)
                    act.activation(probs[:, h % PROBS, cols], probs[:, h % PROBS, cols], ACT.Exp,
                                   bias=neg_max[:, h, t:t + 1], scale=-1.0,
                                   accum_out=denom[:, h, t:t + 1]).then_inc(exp_done, 1)

            def read_probs_t(h):
                act.wait_ge(pt_done, h + 1)
                if h >= PROBS_T:
                    act.wait_ge(pv_done, (h - PROBS_T) // 2 + 1)
                act.activation(probs_t[:, h % PROBS_T, :], bank[PT_BANK][:, 0:BLK],
                               ACT.Copy).then_inc(pt_read, 1)

            def read_qk(n):
                act.wait_ge(chunk_used, chunks_to(n // 2))
                act.activation(unrotated[:, n, :, :], bank[BLOCK_BANKS[n // 2][n % 2]][:, :].rearrange(
                    "p (f n) -> p f n", f=2), ACT.Copy).then_inc(qk_read, 1)

            def read_v():
                act.wait_ge(chunk_used, chunks_to(V))
                act.wait_ge(rstd_done, 1)
                for t in range(TT):
                    act.activation(v[:, t, :], bank[BLOCK_BANKS[V % 2][t]][:, :], ACT.Copy,
                                   scale=rstd[:, t:t + 1]).then_inc(v_done, 1)

            def read_attn(pair):
                act.wait_ge(pv_done, pair + 1)
                act.activation(attn[:, pair, :], bank[PV_BANK][:, 0:SEQ], ACT.Copy).then_inc(pv_read, 1)

            def sigmoids(n):
                act.wait_ge(gate_done, 2 * (n + 1))
                if n > 0:
                    act.wait_ge(mixed_done, GROUPS)
                act.activation(sigm[:, :, :], gate[:, :, :], ACT.Sigmoid).then_inc(sigm_done, 1)

            def split_mixed_hi(k):
                act.wait_ge(mixed_done, k + 1)
                act.activation(mixed_hi[:, k, :], mixed[:, k, :], ACT.Copy).then_inc(mixed_hi_done, 1)

            act.dma_start(gain_col[:, :], gain).then_inc(gain_loaded, 16)
            act.wait_ge(memset_done, 4)
            act.activation(warm[:, :], neg_half[:, :], ACT.Exp)
            act.wait_ge(gain_loaded, 16)
            split_x_hi(0)
            split_piece_hi(0)
            split_piece_hi(1)
            for k in range(1, KT):
                split_x_hi(k)
                split_piece_hi(k + 1)
            for s in range(STEPS):
                if s in READ_QK_AT:
                    read_qk(READ_QK_AT.index(s))
                if s == READ_V_AT:
                    read_v()
                if s in SPLIT_HEADS_AT:
                    split_heads_hi(SPLIT_HEADS_AT.index(s))
                if (h := head_at(exp_at, s)) is not None:
                    exps(h)
                if (h := head_at(evacuate_at, s)) is not None:
                    read_probs_t(h)
                if (pair := pair_at(read_attn_at, s)) is not None:
                    read_attn(pair)
                if s == SIGMOID_AT[0]:
                    sigmoids(0)
                if s in SPLIT_MIXED_HI_AT:
                    first = GROUPS * SPLIT_MIXED_HI_AT.index(s)
                    for k in range(first, first + GROUPS):
                        split_mixed_hi(k)
                if s % 2 == 0 and (c := (s + AHEAD) // 2) < CHUNKS:
                    split_hi(c)
                if s == SQUARES_AT:
                    squares(0)
                    squares(1)
                if s == SIGMOID_AT[1]:
                    sigmoids(1)

            def squares_of_part(t, i):
                at, size, _ = OUT_PARTS[t][i]
                act.wait_ge(added_done, len(OUT_PARTS[0]) * t + i + 1)
                act.activation(square_out[t][:, at:at + size], res[:, t, at:at + size], ACT.Square,
                               scale=D ** -0.5, accum_out=out_square[:, t, i:i + 1]).then_inc(out_square_done, 1)

            def scale_tile(t, columns):
                act.wait_ge(gained_done, len(OUT_PARTS[0]) * (t + 1))
                act.wait_ge(out_rstd_done, t + 1)
                act.activation(res[:, t, 0:columns], gained[:, t, 0:columns], ACT.Copy,
                               scale=out_rstd[:, t:t + 1]).then_inc(scaled_act_done, 1)

            squares_of_part(0, 0)
            squares_of_part(0, 1)
            scale_tile(0, D)
            squares_of_part(1, 0)
            squares_of_part(1, 1)
            scale_tile(1, SCALED_BY_ACT)
            act.wait_ge(scaled_act_done, TT)
            act.dma_start(out[P:, 0:SCALED_BY_ACT], res[:, 1, 0:SCALED_BY_ACT]).then_inc(stored, 16)

        @block.vector
        def _(dve):
            def split_lo(c):
                dve.wait_ge(w_hi_done, splits(c))
                if c >= SPLIT:
                    dve.wait_ge(chunk_used, c - SPLIT + 1)
                dve.tensor_tensor(w_lo[:, c % SPLIT, :], w_raw[:, c % RAW, :], w_hi[:, c % SPLIT, :].bitcast(fp32),
                                  ALU.subtract).then_inc(w_lo_done, 1)

            def split_piece_lo(i):
                c, at, size = PIECES[i]
                dve.wait_ge(w_hi_done, i + 1)
                dve.tensor_tensor(w_lo[:, c, at:at + size], w_raw[:, c, at:at + size],
                                  w_hi[:, c, at:at + size].bitcast(fp32), ALU.subtract).then_inc(w_lo_done, 1)

            def split_x_lo(k):
                dve.wait_ge(x_hi_done, k + 1)
                dve.scalar_tensor_tensor(x_lo[:, k, :], xt[:, k, :], gain_col[:, k:k + 1],
                                         x_hi[:, k, :].bitcast(fp32), ALU.mult,
                                         ALU.subtract).then_inc(x_lo_done, 1)

            def make_diag():
                dve.wait_ge(rstd_done, 1)
                dve.wait_ge(consts_done, 2)
                for t in range(TT):
                    dve.tensor_scalar(rstd_diag[:, t * P:(t + 1) * P], ident[:, :], rstd[:, t:t + 1],
                                      None, ALU.mult).then_inc(diag_done, 1)

            def make_tables():
                dve.wait_ge(bcast_done, 1)
                dve.tensor_copy(rstd_row[:, :], bank[PV_BANK][:, 0:SEQ]).then_inc(rstd_row_done, 1)
                dve.wait_ge(rstd_row_done, 1)
                dve.wait_ge(table_loaded, 16)
                dve.tensor_tensor(rope_scaled[:, :, :], table[:, :, :], over(rstd_row, 2),
                                  ALU.mult).then_inc(tables_done, 1)

            def over(row, n):
                return row[:, :].unsqueeze(1).broadcast_to([P, n, SEQ])

            def rotate(n):
                read = 2 * (n % 2) + n // 2
                src = unrotated[:, read, :, :]
                dve.wait_ge(qk_read, read + 1)
                dve.wait_ge(tables_done, 1)
                if n > 0:
                    dve.wait_ge(roped_done, n)
                dve.tensor_tensor(rope_sin[:, :, :], src, rope_scaled[:, 1:2, :].broadcast_to([P, 2, SEQ]),
                                  ALU.mult).then_inc(products_done, 1)
                dve.wait_ge(products_done, 2 * n + 1)
                dve.tensor_tensor(src, src, rope_scaled[:, 0:1, :].broadcast_to([P, 2, SEQ]),
                                  ALU.mult).then_inc(products_done, 1)
                dve.wait_ge(products_done, 2 * (n + 1))
                dve.tensor_tensor(roped[:, n, 0, :], src[:, 0, :], rope_sin[:, 1, :], ALU.subtract)
                dve.tensor_tensor(roped[:, n, 1, :], src[:, 1, :], rope_sin[:, 0, :],
                                  ALU.add).then_inc(roped_done, 1)

            def split_heads_lo(n):
                pairs = slice(2 * n, 2 * n + 2)
                dve.wait_ge(qk_moved[2 * n], 16 * 4)
                dve.wait_ge(qk_moved[2 * n + 1], 16 * 4)
                dve.wait_ge(heads_hi_done, 2 * n + 1)
                dve.tensor_tensor(q_lo[:, pairs, :], qk[:, 0, pairs, P:SEQ], q_hi[:, pairs, :].bitcast(fp32),
                                  ALU.subtract).then_inc(heads_lo_done, 1)
                dve.wait_ge(heads_hi_done, 2 * n + 2)
                dve.tensor_tensor(k_lo[:, pairs, :], qk[:, 1, pairs, :], k_hi[:, pairs, :].bitcast(fp32),
                                  ALU.subtract).then_inc(heads_lo_done, 1)

            def mask_and_max(h):
                dve.wait_ge(scores_done, h + 1)
                if h >= PROBS:
                    dve.wait_ge(pt_done, h - PROBS + 1)
                b = bank[SCORES_BANK[h % 2]]
                for t in range(TT):
                    cols, m = (slice(0, P), slice(P, 2 * P)) if t == 0 else (slice(P, BLK), slice(0, 2 * P))
                    dve.tensor_tensor_reduce(out=probs[:, h % PROBS, cols], in0=b[:, cols], in1=mask[:, m],
                                             scale=-SCALE, scalar=-MASKED, op0=ALU.add, op1=ALU.min,
                                             accum_out=neg_max[:, h, t:t + 1]).then_inc(masked_done, 1)

            def normalise(h):
                dve.wait_ge(exp_done, TT * (h + 1))
                dve.reciprocal(denom_recip[:, h, :], denom[:, h, :]).then_inc(recip_done, 1)
                dve.wait_ge(recip_done, h + 1)
                for t in range(TT):
                    cols = slice(0, P) if t == 0 else slice(P, BLK)
                    dve.tensor_scalar(probs[:, h % PROBS, cols], probs[:, h % PROBS, cols],
                                      denom_recip[:, h, t:t + 1], None, ALU.mult).then_inc(norm_done, 1)

            def read_rows(place, dst, done):
                dve.wait_ge(chunk_used, chunks_to(place))
                for i, b in enumerate(BLOCK_BANKS[place % 2]):
                    dve.tensor_tensor(dst[:, 2 * i:2 * i + 2, :],
                                      bank[b][:, :].rearrange("p (f n) -> p f n", f=2), over(rstd_row, 2),
                                      ALU.mult).then_inc(done, 1)

            sums = (sum_a, sum_b)

            def double(g):
                src, dst, shift = (u_pad if g == 0 else sums[(g - 1) % 2]), sums[g % 2], 1 << g
                lo = 2 * shift - 1
                dve.wait_ge(u_done, 2)
                if g > 0:
                    dve.wait_ge(sums_done, g)
                dve.tensor_tensor(dst[:, g:GROUPS, lo:], src[:, g:GROUPS, lo:],
                                  src[:, g:GROUPS, lo - shift:PAD + SEQ - shift],
                                  ALU.add).then_inc(sums_done, 1)

            def pool_minus_token(g):
                dve.wait_ge(sums_done, GROUPS)
                dve.wait_ge(pool_consts_loaded, 16 * 4)
                s = sums[g % 2]
                dve.tensor_tensor(edge_mean[:, g, :], s[:, g, PAD:PAD + EDGE], edge_recip[:, g, :],
                                  ALU.mult).then_inc(edge_done, 1)
                dve.scalar_tensor_tensor(pooled[:, g, EDGE:], s[:, g, PAD + EDGE:], 1.0 / WINDOWS[g],
                                         u_pad[:, g, PAD + EDGE:], ALU.mult,
                                         ALU.subtract).then_inc(pooled_done, 1)
                dve.wait_ge(edge_done, g + 1)
                dve.tensor_tensor(pooled[:, g, 0:EDGE], edge_mean[:, g, :], u_pad[:, g, PAD:PAD + EDGE],
                                  ALU.subtract).then_inc(pooled_done, 1)


            def bias_and_gate(g):
                dve.wait_ge(wpool_done, g // 2 + 1)
                dve.wait_ge(gate_done, 2)
                product = bank[POOL_BANKS[g // 2]][:, (g % 2) * SEQ:(g % 2 + 1) * SEQ]
                dve.scalar_tensor_tensor(pooled[:, g, :], product, b_col[:, g:g + 1], gate[:, g, :], ALU.add,
                                         ALU.mult).then_inc(pool_gated, 1)

            def gate_attention():
                dve.wait_ge(pv_read, HEADS // 2)
                dve.wait_ge(gate_done, 4)
                dve.tensor_tensor(attn[:, :, :], attn[:, :, :], gate[:, :, :], ALU.mult).then_inc(attn_gated, 1)

            def mix(k):
                g = k % GROUPS
                if k < GROUPS:
                    dve.wait_ge(sigm_done, 1)
                    dve.wait_ge(pool_gated, g + 1)
                    dve.scalar_tensor_tensor(mixed[:, k, :], pooled[:, g, :], scale_col[:, g:g + 1], sigm[:, g, :],
                                             ALU.mult, ALU.mult).then_inc(mixed_done, 1)
                else:
                    dve.wait_ge(sigm_done, 2)
                    dve.wait_ge(attn_gated, 1)
                    dve.tensor_tensor(mixed[:, k, :], attn[:, g, :], sigm[:, g, :],
                                      ALU.mult).then_inc(mixed_done, 1)

            def split_mixed_lo(k):
                dve.wait_ge(mixed_hi_done, k + 1)
                dve.tensor_tensor(mixed_lo[:, k, :], mixed[:, k, :], mixed_hi[:, k, :].bitcast(fp32),
                                  ALU.subtract).then_inc(mixed_lo_done, 1)

            dve.memset(ones[:, :], 1.0).then_inc(ones_done, 1)
            dve.wait_ge(gain_loaded, 16)
            split_x_lo(0)
            split_piece_lo(0)
            split_piece_lo(1)
            for k in range(1, KT):
                split_x_lo(k)
                split_piece_lo(k + 1)
            for s in range(STEPS):
                if s == DIAG_AT:
                    make_diag()
                if s == TABLES_AT:
                    make_tables()
                if s in SPLIT_HEADS_AT:
                    split_heads_lo(SPLIT_HEADS_AT.index(s))
                if s in ROTATE_AT:
                    rotate(ROTATE_AT.index(s))
                if (h := head_at(softmax_at, s)) is not None:
                    mask_and_max(h)
                if (h := head_at(normalise_at, s)) is not None:
                    normalise(h)
                if s == READ_U_AT:
                    read_rows(U, u_pad[:, :, PAD:], u_done)
                if s in DOUBLE_AT:
                    double(DOUBLE_AT.index(s))
                if s in POOL_AT:
                    pool_minus_token(POOL_AT.index(s))
                if s == READ_GATE_AT[0]:
                    read_rows(GP, gate, gate_done)
                if s == GATE_BRANCH_AT[0]:
                    for g in range(GROUPS):
                        bias_and_gate(g)
                if s == READ_GATE_AT[1]:
                    dve.wait_ge(pool_gated, GROUPS)
                    dve.wait_ge(sigm_done, 1)
                    read_rows(GA, gate, gate_done)
                if s == GATE_BRANCH_AT[1]:
                    gate_attention()
                if s % 2 == 0 and (c := (s + AHEAD) // 2) < CHUNKS:
                    split_lo(c)
                if s in MIX_AT:
                    first = GROUPS * MIX_AT.index(s)
                    for k in range(first, first + GROUPS):
                        mix(k)
                        if k > first:
                            split_mixed_lo(k - 1)
                    split_mixed_lo(first + GROUPS - 1)

            def add_residual(t, i):
                at, size, b = OUT_PARTS[t][i]
                dve.wait_ge(out_done, len(OUT_PARTS[0]) * t + i + 1)
                dve.tensor_tensor(res[:, t, at:at + size], bank[b][:, 0:size],
                                  res[:, t, at:at + size], ALU.add).then_inc(added_done, 1)

            def apply_gain(t, i):
                at, size, _ = OUT_PARTS[t][i]
                dve.wait_ge(added_done, len(OUT_PARTS[0]) * t + i + 1)
                dve.tensor_tensor(gained[:, t, at:at + size], res[:, t, at:at + size], final_row[:, at:at + size],
                                  ALU.mult).then_inc(gained_done, 1)

            def add_means(t, target):
                dve.wait_ge(out_square_done, 2 * (t + 1))
                return dve.tensor_scalar(target, out_square[:, t, 0:1], out_square[:, t, 1:2], EPS, ALU.add, ALU.add)

            dve.wait_ge(final_loaded, 16)
            for i in range(2):
                add_residual(0, i)
                apply_gain(0, i)
            add_means(0, out_mean[:, 0:1]).then_inc(out_mean_done, 1)
            for i in range(2):
                add_residual(1, i)
                apply_gain(1, i)
            add_means(1, mean_others[:, :]).then_inc(mean_others_done, 1)
            add_residual(1, 2)
            dve.wait_ge(added_done, 5)
            dve.wait_ge(mean_others_done, 1)
            at = OUT_PARTS[1][2][0]
            dve.tensor_tensor_reduce(out=last_square, in0=res[:, 1, at:], in1=res[:, 1, at:],
                                     scale=1.0 / D, scalar=mean_others[:, 0:1], op0=ALU.mult, op1=ALU.add,
                                     accum_out=out_mean[:, 1:2]).then_inc(out_mean_done, 1)
            apply_gain(1, 2)
            dve.wait_ge(gained_done, 5)
            dve.wait_ge(out_rstd_done, 2)
            for lo, hi in SCALED_BY_DVE:
                dve.tensor_scalar(res[:, 1, lo:hi], gained[:, 1, lo:hi], out_rstd[:, 1:2], None,
                                  ALU.mult).then_inc(scaled_done, 1)

        @block.tensor
        def _(pe):
            PASSES = ((w_hi, 0), (w_hi, 1), (w_lo, 0))

            def wait_for_banks(place):
                if place == V:
                    pe.wait_ge(qk_read, 2)
                if place == U:
                    pe.wait_ge(qk_read, 4)
                if place == GP:
                    pe.wait_ge(v_done, TT)
                if place == GA:
                    pe.wait_ge(u_done, 2)

            def project(s):
                place, k, c = s // KT, s % KT, s // 2
                if k == 0:
                    wait_for_banks(place)
                columns = ((0, 1), (2, 3)) if s == 0 else (range(4),)
                for group in columns:
                    for n, (w, lo) in enumerate(PASSES):
                        if c < FINE:
                            to = splits_to(c, k % 2 * WIDTH + group[-1] * P)
                            pe.wait_ge(w_lo_done if n == 2 else w_hi_done, to)
                        elif k % 2 == 0:
                            pe.wait_ge(w_lo_done if n == 2 else w_hi_done, splits(c))
                        if place == Q and n < 2:
                            pe.wait_ge((x_hi_done, x_lo_done)[n], k + 1)
                        act, tile = (x_hi, x_lo)[lo], w[:, c % SPLIT, k % 2 * WIDTH:(k % 2 + 1) * WIDTH]
                        first, last = k == 0 and n == 0, k == KT - 1 and n == 2
                        if place == V:
                            for t in range(TT):
                                mm = pe.matmul(bank[BLOCK_BANKS[0][t]][:, :], act[:, k, t * P:(t + 1) * P], tile,
                                               start=first, stop=last, skip_group_check=True)
                            continue
                        for i in group:
                            mm = pe.matmul(bank[BLOCK_BANKS[place % 2][i // 2]][:, (i % 2) * SEQ:(i % 2 + 1) * SEQ],
                                           tile[:, i * P:(i + 1) * P], act[:, k, :], start=first and i % 2 == 0,
                                           stop=last, skip_group_check=True)
                return mm

            def project_out(k, t, n, parts):
                c, (w, lo) = IN_CHUNKS + k, PASSES[n]
                pe.wait_ge(w_lo_done if n == 2 else w_hi_done, splits(c))
                if n < 2:
                    pe.wait_ge((mixed_hi_done, mixed_lo_done)[n], k + 1)
                for at, size, b in parts:
                    mm = pe.matmul(bank[b][:, 0:size], (mixed_hi, mixed_lo)[lo][:, k, t * P:(t + 1) * P],
                                   w[:, c % SPLIT, at:at + size], start=(k == 0 and n == 0),
                                   stop=(k == KT - 1 and n == 2), skip_group_check=True)
                return mm

            def scores(pair):
                n, half = pair // 2, (slice(0, HEAD_DIM), slice(HEAD_DIM, P))
                pe.wait_ge(qk_moved[2 * n], 16 * 4)
                pe.wait_ge(qk_moved[2 * n + 1], 16 * 4)
                if pair > 0:
                    pe.wait_ge(masked_done, TT * 2 * pair)
                for i, at in enumerate(half):
                    pe.matmul(bank[SCORES_BANK[i]][:, 0:P], qk[at, 0, pair, 0:P], qk[at, 1, pair, 0:P],
                              start=True, stop=True)
                pe.wait_ge(heads_lo_done, 2 * (n + 1))
                for step, (q_part, k_part) in enumerate(((q_hi, k_hi), (q_hi, k_lo), (q_lo, k_hi))):
                    for i, at in enumerate(half):
                        mm = pe.matmul(bank[SCORES_BANK[i]][:, P:BLK], q_part[at, pair, :], k_part[at, pair, :],
                                       start=(step == 0), stop=(step == 2))
                        if step == 2:
                            mm.then_inc(scores_done, 1)

            def transpose(h):
                pe.wait_ge(norm_done, TT * (h + 1))
                if h > 0:
                    pe.wait_ge(pt_read, h)
                for i in range(3):
                    mm = pe.transpose(bank[PT_BANK][:, i * P:(i + 1) * P],
                                      probs[:, h % PROBS, i * P:(i + 1) * P], ident[:, :])
                mm.then_inc(pt_done, 1)

            def attend(pair):
                pe.wait_ge(v_done, TT)
                pe.wait_ge(pt_read, 2 * pair + 2)
                if pair > 0:
                    pe.wait_ge(pv_read, pair)
                for t, first, at in ((0, 0, 0), (1, P, SEQ)):
                    for h in (2 * pair, 2 * pair + 1):
                        rows = slice(HEAD_DIM * (h % 2), HEAD_DIM * (h % 2 + 1))
                        mm = pe.matmul(bank[PV_BANK][rows, first:SEQ], v[:, t, h * HEAD_DIM:(h + 1) * HEAD_DIM],
                                       probs_t[:, h % PROBS_T, at:at + SEQ - first], start=(t == 0),
                                       stop=(t == 1))
                mm.then_inc(pv_done, 1)

            def broadcast_rstd():
                for t in range(TT):
                    pe.wait_ge(diag_done, t + 1)
                    mm = pe.matmul(bank[PV_BANK][:, t * P:(t + 1) * P], ones[:, :],
                                   rstd_diag[:, t * P:(t + 1) * P], start=True, stop=True)
                mm.then_inc(bcast_done, 1)

            def pool_weights(i):
                pe.wait_ge(gate_done, i + 1)
                pe.wait_ge(pool_consts_loaded, 16 * 4)
                for g in (2 * i, 2 * i + 1):
                    pe.wait_ge(pooled_done, 2 * (g + 1))
                    mm = pe.matmul(bank[POOL_BANKS[i]][:, (g % 2) * SEQ:(g % 2 + 1) * SEQ], wp[:, g, :],
                                   pooled[:, g, :], start=True, stop=True)
                mm.then_inc(wpool_done, 1)

            pe.wait_ge(ones_done, 1)
            for _ in range(WARM_UP):
                pe.matmul(bank[PT_BANK][:, 0:P], ones[:, :], ones[:, :], start=True, stop=True)
            for s in range(OUT_STEP):
                mm = project(s)
                if s % 2 == 1:
                    mm.then_inc(chunk_used, 1)
                if s == BROADCAST_AT:
                    broadcast_rstd()
                if (pair := pair_at(scores_at, s)) is not None:
                    scores(pair)
                if (h := head_at(transpose_at, s)) is not None:
                    transpose(h)
                if (pair := pair_at(attend_at, s)) is not None:
                    attend(pair)
                if s in POOL_WEIGHTS_AT:
                    pool_weights(POOL_WEIGHTS_AT.index(s))
            pe.wait_ge(pool_gated, GROUPS)
            for k in range(KT - TAIL):
                for t in range(TT):
                    if k == 0 and t == 1:
                        pe.wait_ge(pv_read, HEADS // 2)
                    for n in range(len(PASSES)):
                        mm = project_out(k, t, n, OUT_PARTS[t])
                mm.then_inc(chunk_used, 1)
            for t in range(TT):
                for part in OUT_PARTS[t]:
                    for k in range(KT - TAIL, KT):
                        for n in range(len(PASSES)):
                            mm = project_out(k, t, n, (part,))
                    mm.then_inc(out_done, 1)


def kernel(**inputs):
    import concourse.bacc as bacc
    from concourse.bass_utils import run_bass_kernel_spmd

    inputs = {name: np.asarray(a) for name, a in inputs.items()}
    x = np.ascontiguousarray(inputs["x"])[0]
    arrays = {
        "x": x,
        "x_t": np.ascontiguousarray(x.T),
        "gain": np.ascontiguousarray(inputs["norm_gain"][0].reshape(KT, P).T),
        "w_in": rotary_columns_together(inputs["w_in"][0]),
        "w_pool": np.ascontiguousarray(inputs["w_pool"][0]),
        "b_pool": np.ascontiguousarray(inputs["b_pool"][0].T),
        "pool_scale": np.ascontiguousarray(inputs["pool_scale"][0].reshape(GROUPS, P).T),
        "w_out": np.ascontiguousarray(inputs["w_out"][0]),
        "final_gain": np.ascontiguousarray(inputs["final_gain"]),
        "rope_table": rope_constants(),
        "edge_table": edge_constants(),
    }
    nc = bacc.Bacc("TRN2", target_bir_lowering=False, num_devices=1)
    args = [nc.dram_tensor("in_" + name, a.shape, mybir.dt.from_np(a.dtype), kind="ExternalInput").ap()
            for name, a in arrays.items()]
    out = nc.dram_tensor("out_dram", (SEQ, D), mybir.dt.float32, kind="ExternalOutput").ap()
    hymba_kernel(nc, *args, out)
    r = run_bass_kernel_spmd(nc, [{"in_" + name: a for name, a in arrays.items()}], core_ids=[0])
    return r.results[0]["out_dram"].reshape(1, SEQ, D)


def rotary_columns_together(w_in):
    qk = w_in[:, :2 * WIDTH].reshape(D, 2, 2, 4, 2, HALF).transpose(0, 1, 2, 4, 3, 5)
    return np.ascontiguousarray(np.concatenate([qk.reshape(D, 2 * WIDTH), w_in[:, 2 * WIDTH:]], axis=1))


def rope_constants():
    inv_freq = (np.float32(1.0) / np.float32(THETA) ** (np.arange(0, HEAD_DIM, 2, dtype=np.float32)
                                                        / np.float32(HEAD_DIM))).astype(np.float32)
    angle = inv_freq[:, None] * np.arange(SEQ, dtype=np.float32)[None, :]
    both = np.stack([np.cos(angle), np.sin(angle)], axis=1).astype(np.float32)
    return np.ascontiguousarray(np.tile(both, (P // HALF, 1, 1)))


def edge_constants():
    counts = np.minimum(np.arange(1, EDGE + 1)[None, :], np.array(WINDOWS)[:, None])
    one = (np.float32(1.0) / counts.astype(np.float32)).astype(np.float32)
    return np.ascontiguousarray(np.broadcast_to(one, (P, GROUPS, EDGE)))
```
